# Optimizing a Trainium2 kernel written in Bass

```python
import math
import jax, jax.numpy as jnp
from jax import lax
import numpy as np

D_MODEL = 1024
BATCH = 1
SEQ = 256
DEPTH = 4

N_MIXERS = 3
N_LAYERS_A = (DEPTH + 2) // 3
N_LAYERS_B = (DEPTH + 1) // 3
N_LAYERS_C = DEPTH // 3

A_HEADS = 8
A_DK = 128
A_DV = 128
A_QK_W = A_HEADS * A_DK
A_V_W = A_HEADS * A_DV
A_CONV = 4
A_CHUNK = 64
A_IN_W = 2 * A_QK_W + 2 * A_V_W + 2 * A_HEADS

B_DH = 64
B_HEADS = D_MODEL // (2 * B_DH)
B_BLOCK = 128
REL_BUCKETS = 32
REL_MAX_DIST = 128

C_CHUNK = 128
C_HALF = 2 * D_MODEL
C_GROUPS = 8
C_GW = C_HALF // C_GROUPS

N_EXPERTS = 16
N_GROUPS = 4
EXPERTS_PER_GROUP = N_EXPERTS // N_GROUPS
TOP_K = 2
D_EXPERT = 512

DN_ALPHA = (2 * DEPTH) ** 0.25
DN_BETA = (8 * DEPTH) ** -0.25
EPS = 1e-5

kernel_name = "hybrid_deltanet_diffattn_gmlp_groupmoe"

def layer_norm(x, g, b):
    xf = x.astype(jnp.float32)
    mu = jnp.mean(xf, -1, keepdims=True)
    var = jnp.mean(jnp.square(xf - mu), -1, keepdims=True)
    return ((xf - mu) * lax.rsqrt(var + EPS) * g + b).astype(x.dtype)

def rms_norm(x, g):
    xf = x.astype(jnp.float32)
    return (xf * lax.rsqrt(jnp.mean(xf * xf, -1, keepdims=True) + EPS) * g).astype(x.dtype)

def l2norm(x):
    xf = x.astype(jnp.float32)
    return xf * lax.rsqrt(jnp.sum(xf * xf, -1, keepdims=True) + 1e-6)

def causal_short_conv(x, w):
    kw = w.shape[0]
    s = x.shape[1]
    xp = jnp.pad(x, ((0, 0), (kw - 1, 0), (0, 0)))
    y = xp[:, 0:s] * w[0]
    for j in range(1, kw):
        y = y + xp[:, j:j + s] * w[j]
    return y

def gated_delta_rule(q, k, v, g, beta):
    b, s, h, dk = q.shape
    dv = v.shape[-1]
    c = A_CHUNK
    n = s // c
    f32 = jnp.float32

    def to_chunks(t):
        t = t.astype(f32).reshape((b, n, c, h) + t.shape[3:])
        return jnp.moveaxis(t, 3, 1)

    q = to_chunks(q) * dk ** -0.5
    k = to_chunks(k)
    v = to_chunks(v)
    beta = to_chunks(beta)
    g = jnp.cumsum(to_chunks(g), axis=-1)
    idx = jnp.arange(c)
    causal = idx[:, None] >= idx[None, :]
    strict = idx[:, None] > idx[None, :]
    decay = jnp.exp(jnp.where(causal, g[..., :, None] - g[..., None, :], -jnp.inf))
    kb = k * beta[..., None]
    a_mat = jnp.where(strict, jnp.einsum('bhncd,bhnmd->bhncm', kb, k) * decay, 0.0)
    rhs = jnp.concatenate([v * beta[..., None], kb * jnp.exp(g)[..., None]], axis=-1)
    sol = lax.linalg.triangular_solve(a_mat + jnp.eye(c, dtype=f32), rhs,
                                      left_side=True, lower=True, unit_diagonal=True)
    u, w = sol[..., :dv], sol[..., dv:]
    attn = jnp.einsum('bhncd,bhnmd->bhncm', q, k) * decay
    q_dec = q * jnp.exp(g)[..., None]
    g_last = g[..., -1]
    k_dec = k * jnp.exp(g_last[..., None] - g)[..., None]

    def step(state, xs):
        attn_c, qd, kd, u_c, w_c, gl = xs
        v_new = u_c - jnp.einsum('bhck,bhkv->bhcv', w_c, state)
        o = jnp.einsum('bhck,bhkv->bhcv', qd, state) + jnp.einsum('bhcm,bhmv->bhcv', attn_c, v_new)
        state = state * jnp.exp(gl)[..., None, None] + jnp.einsum('bhck,bhcv->bhkv', kd, v_new)
        return state, o

    xs = tuple(jnp.moveaxis(t, 2, 0) for t in (attn, q_dec, k_dec, u, w, g_last))
    s0 = jnp.zeros((b, h, dk, dv), f32)
    _, o = lax.scan(step, s0, xs)
    return jnp.transpose(o, (1, 0, 3, 2, 4)).reshape(b, s, h, dv)

def gated_deltanet_mixer(x, w_in, conv_w, a_log, dt_bias, norm_g, w_out):
    b, s, _ = x.shape
    proj = x @ w_in
    qkv, gate, a_raw, b_raw = jnp.split(
        proj, [2 * A_QK_W + A_V_W, 2 * A_QK_W + 2 * A_V_W, 2 * A_QK_W + 2 * A_V_W + A_HEADS], axis=-1)
    qkv = jax.nn.silu(causal_short_conv(qkv, conv_w))
    q, k, v = jnp.split(qkv, [A_QK_W, 2 * A_QK_W], axis=-1)
    q = l2norm(q.reshape(b, s, A_HEADS, A_DK))
    k = l2norm(k.reshape(b, s, A_HEADS, A_DK))
    v = v.reshape(b, s, A_HEADS, A_DV)
    g = -jnp.exp(a_log.astype(jnp.float32)) * jax.nn.softplus(a_raw.astype(jnp.float32) + dt_bias)
    beta = jax.nn.sigmoid(b_raw.astype(jnp.float32))
    o = gated_delta_rule(q, k, v, g, beta)
    o = rms_norm(o, norm_g) * jax.nn.silu(gate.reshape(b, s, A_HEADS, A_DV).astype(jnp.float32))
    return o.reshape(b, s, A_V_W).astype(x.dtype) @ w_out

def rel_position_bucket(rel):
    n = jnp.maximum(rel, 0)
    max_exact = REL_BUCKETS // 2
    large = max_exact + (jnp.log(jnp.maximum(n, 1).astype(jnp.float32) / max_exact)
                         / math.log(REL_MAX_DIST / max_exact) * (REL_BUCKETS - max_exact)).astype(jnp.int32)
    large = jnp.minimum(large, REL_BUCKETS - 1)
    return jnp.where(n < max_exact, n, large)

def diff_attention_mixer(x, w_in, lam, norm_g, w_out, rel_bias, lambda_init):
    b, s, _ = x.shape
    q, k, v = jnp.split(x @ w_in, 3, axis=-1)
    q = q.reshape(b, s, B_HEADS, 2, B_DH)
    k = k.reshape(b, s, B_HEADS, 2, B_DH)
    v = v.reshape(b, s, B_HEADS, 2 * B_DH)
    lamf = lam.astype(jnp.float32)
    lam_full = jnp.exp(jnp.sum(lamf[0] * lamf[1])) - jnp.exp(jnp.sum(lamf[2] * lamf[3])) + lambda_init
    nblk = s // B_BLOCK
    qb = jnp.moveaxis(q.reshape(b, nblk, B_BLOCK, B_HEADS, 2, B_DH), 1, 0)
    kpos = jnp.arange(s)

    def block(args):
        qi, q_blk = args
        qpos = qi * B_BLOCK + jnp.arange(B_BLOCK)
        rel = qpos[:, None] - kpos[None, :]
        bias = rel_bias.astype(jnp.float32)[rel_position_bucket(rel)]
        logits = (jnp.einsum('bqhmd,bkhmd->bhmqk', q_blk, k).astype(jnp.float32) * B_DH ** -0.5
                  + jnp.transpose(bias, (2, 0, 1))[None, :, None])
        logits = jnp.where(rel >= 0, logits, -jnp.inf)
        p = jax.nn.softmax(logits, axis=-1)
        attn = p[:, :, 0] - lam_full * p[:, :, 1]
        return jnp.einsum('bhqk,bkhd->bqhd', attn.astype(v.dtype), v)

    o = lax.map(block, (jnp.arange(nblk), qb))
    o = jnp.moveaxis(o, 0, 1).reshape(b, s, B_HEADS, 2 * B_DH)
    o = rms_norm(o, norm_g) * (1.0 - lambda_init)
    return o.reshape(b, s, D_MODEL).astype(x.dtype) @ w_out

def chunked_gmlp_mixer(x, w_in, ln_g, ln_b, w_s, b_s, w_out):
    b, s, _ = x.shape
    z = jax.nn.gelu(x @ w_in, approximate=False)
    u, v = jnp.split(z, 2, axis=-1)
    v = layer_norm(v, ln_g, ln_b)
    n = s // C_CHUNK
    v = v.reshape(b, n, C_CHUNK, C_GROUPS, C_GW)
    idx = jnp.arange(C_CHUNK)
    w_causal = jnp.where(idx[:, None] >= idx[None, :], w_s, 0.0)
    mixed = jnp.einsum('gts,bnsgc->bntgc', w_causal, v) + jnp.transpose(b_s)[:, :, None]
    return (u * mixed.reshape(b, s, C_HALF)) @ w_out

def grouped_moe(x, w_router, router_bias, w1, w3, w2):
    b, s, d = x.shape
    t = x.reshape(b * s, d)
    scores = jax.nn.sigmoid((t @ w_router).astype(jnp.float32))
    sel = scores + router_bias.astype(jnp.float32)
    grp_score = jnp.sum(lax.top_k(sel.reshape(-1, N_GROUPS, EXPERTS_PER_GROUP), TOP_K)[0], -1)
    best = jnp.argmax(grp_score, -1)
    in_group = (jnp.arange(N_EXPERTS) // EXPERTS_PER_GROUP)[None, :] == best[:, None]
    _, top_idx = lax.top_k(jnp.where(in_group, sel, -jnp.inf), TOP_K)
    top_w = jnp.take_along_axis(scores, top_idx, -1)
    top_w = top_w / jnp.sum(top_w, -1, keepdims=True)
    gates = jnp.einsum('tk,tke->te', top_w, jax.nn.one_hot(top_idx, N_EXPERTS, dtype=jnp.float32))
    out = jnp.zeros_like(t)
    for e in range(N_EXPERTS):
        h = jax.nn.silu(t @ w1[e]) * (t @ w3[e])
        out = out + gates[:, e:e + 1].astype(t.dtype) * (h @ w2[e])
    return out.reshape(b, s, d)

def setup_inputs(seed: int = 0) -> dict:
    key = jax.random.key(seed)
    ks = iter(jax.random.split(key, 40))
    f32 = jnp.float32

    def nrm(shape, scale):
        return jax.random.normal(next(ks), shape, f32) * scale

    def gain(shape):
        return 1.0 + nrm(shape, 0.02)

    nA, nB, nC = N_LAYERS_A, N_LAYERS_B, N_LAYERS_C
    a_decay = jax.random.uniform(next(ks), (nA, A_HEADS), f32, 1.0, 16.0)
    dt = jnp.exp(jax.random.uniform(next(ks), (nA, A_HEADS), f32, math.log(1e-3), math.log(1e-1)))
    return {
        "x": nrm((BATCH, SEQ, D_MODEL), 1.0),
        "ln_mix_g": gain((DEPTH, D_MODEL)),
        "ln_mix_b": nrm((DEPTH, D_MODEL), 0.02),
        "ln_ffn_g": gain((DEPTH, D_MODEL)),
        "ln_ffn_b": nrm((DEPTH, D_MODEL), 0.02),
        "a_w_in": nrm((nA, D_MODEL, A_IN_W), D_MODEL ** -0.5),
        "a_conv": nrm((nA, A_CONV, 2 * A_QK_W + A_V_W), A_CONV ** -0.5),
        "a_a_log": jnp.log(a_decay),
        "a_dt_bias": dt + jnp.log(-jnp.expm1(-dt)),
        "a_norm_g": gain((nA, A_DV)),
        "a_w_out": nrm((nA, A_V_W, D_MODEL), A_V_W ** -0.5 * DN_BETA),
        "b_w_in": nrm((nB, D_MODEL, 3 * D_MODEL), D_MODEL ** -0.5),
        "b_lambda": nrm((nB, 4, B_DH), 0.1),
        "b_norm_g": gain((nB, 2 * B_DH)),
        "b_w_out": nrm((nB, D_MODEL, D_MODEL), D_MODEL ** -0.5 * DN_BETA),
        "rel_bias": nrm((REL_BUCKETS, B_HEADS), 0.2),
        "c_w_in": nrm((nC, D_MODEL, 2 * C_HALF), D_MODEL ** -0.5),
        "c_ln_g": gain((nC, C_HALF)),
        "c_ln_b": nrm((nC, C_HALF), 0.02),
        "c_w_s": nrm((nC, C_GROUPS, C_CHUNK, C_CHUNK), C_CHUNK ** -0.5),
        "c_b_s": gain((nC, C_GROUPS, C_CHUNK)),
        "c_w_out": nrm((nC, C_HALF, D_MODEL), C_HALF ** -0.5 * DN_BETA),
        "w_router": nrm((D_MODEL, N_EXPERTS), D_MODEL ** -0.5),
        "router_bias": nrm((N_EXPERTS,), 0.01),
        "e_w1": nrm((DEPTH, N_EXPERTS, D_MODEL, D_EXPERT), D_MODEL ** -0.5),
        "e_w3": nrm((DEPTH, N_EXPERTS, D_MODEL, D_EXPERT), D_MODEL ** -0.5),
        "e_w2": nrm((DEPTH, N_EXPERTS, D_EXPERT, D_MODEL), D_EXPERT ** -0.5 * DN_BETA),
    }

def reference(x, ln_mix_g, ln_mix_b, ln_ffn_g, ln_ffn_b,
              a_w_in, a_conv, a_a_log, a_dt_bias, a_norm_g, a_w_out,
              b_w_in, b_lambda, b_norm_g, b_w_out, rel_bias,
              c_w_in, c_ln_g, c_ln_b, c_w_s, c_b_s, c_w_out,
              w_router, router_bias, e_w1, e_w3, e_w2):
    h = x
    for i in range(DEPTH):
        kind, j = i % N_MIXERS, i // N_MIXERS
        if kind == 0:
            y = gated_deltanet_mixer(h, a_w_in[j], a_conv[j], a_a_log[j], a_dt_bias[j],
                                     a_norm_g[j], a_w_out[j])
        elif kind == 1:
            lambda_init = 0.8 - 0.6 * math.exp(-0.3 * i)
            y = diff_attention_mixer(h, b_w_in[j], b_lambda[j], b_norm_g[j], b_w_out[j],
                                     rel_bias, lambda_init)
        else:
            y = chunked_gmlp_mixer(h, c_w_in[j], c_ln_g[j], c_ln_b[j], c_w_s[j], c_b_s[j], c_w_out[j])
        h = layer_norm(DN_ALPHA * h + y, ln_mix_g[i], ln_mix_b[i])
        m = grouped_moe(h, w_router, router_bias, e_w1[i], e_w3[i], e_w2[i])
        h = layer_norm(DN_ALPHA * h + m, ln_ffn_g[i], ln_ffn_b[i])
    return h


_drawn_inputs = setup_inputs


def setup_inputs(seed=0):
    import zlib

    import numpy as np

    out = dict(_drawn_inputs(seed))
    spreads = {}
    factors = {'a_norm_g': 2.977, 'b_norm_g': 3.091, 'c_ln_g': 21.365, 'c_ln_b': 46.419, 'c_b_s': 14.085}
    for name, (base, spread) in spreads.items():
        noise = np.random.default_rng([zlib.crc32(name.encode()), seed]).standard_normal(out[name].shape)
        drawn = base * np.exp(spread * noise) if base else spread * noise
        out[name] = __import__('jax').numpy.asarray(drawn.astype(out[name].dtype))
    for name, factor in factors.items():
        out[name] = (out[name] * factor).astype(out[name].dtype)
    return out
```

```python
import math
from contextlib import ExitStack

import concourse.bass as bass
from concourse import mybir

F32 = mybir.dt.float32
ACT = mybir.ActivationFunctionType
ALU = mybir.AluOpType
AX = mybir.AxisListType.X

P = 128
D = 1024
SEQ = 256
TT = SEQ // P
KC = D // P
DEPTH = 4
HEADS = 8
CHUNK = 64
E = 16
GROUPS = 4
DE = 512
SLOTS = 6
UNIT = 4096
ALPHA = float((2 * DEPTH) ** 0.25)
EPS = 1e-5
L2EPS = 1e-6
BIG = 1e30
LEVELS = 6
REL_BUCKETS = 32
TOEP = 384

C_ID, C_NEG, C_LV, C_CUM, C_BLK, C_TRI, C_CD = 0, 128, 256, 1024, 1152, 1280, 1408
C_SB = C_CD + E
C_OH = C_SB
C_FLIP = C_OH + TOEP
C_ALL = C_FLIP + P

ALL_KINDS = tuple(i % 3 for i in range(DEPTH))


class Turns:

    def __init__(self):
        self.count = [0] * 8
        self.at = {}

    def take(self, bank, *key):
        self.at[key] = (bank, self.count[bank])
        self.count[bank] += 1

    def loop(self, key, per_pass, passes):
        self.at[key] = list(self.count)
        self.count = [c + per_pass * passes for c in self.count]


def plan(kinds, with_moe, w):
    turns, units = Turns(), []

    def unit(src, last):
        units.append((src, last))

    def heads_out(i, w_out):
        for g in range(4):
            turns.take(g, "oT", i, g)
        for nh in range(2):
            for tt in range(TT):
                turns.take(4 + 2 * tt + nh, "y", i, tt, nh)
            unit(w_out[:, nh * 512:(nh + 1) * 512].rearrange("(k p) n -> p k n", p=P), ("y", i, TT - 1, nh))

    turns.take(0, "cols")
    turns.take(1, "relrow")
    for k in range(KC):
        turns.take(k, "ht", 0, k)
    for i, kind in enumerate(kinds):
        j = kinds[:i].count(kind)
        if kind == 0:
            win = w["a_w_in"][j]
            turns.take(0, "ab", i)
            for u in range(6):
                for c in range(4 * u, 4 * u + 4):
                    turns.take(2 + c % 4, "conv", i, c)
                    if c >= 16:
                        turns.take(6 + c % 2, "ss", i, c - 16)
                unit(win[:, u * 512:(u + 1) * 512].rearrange("(k p) n -> p k n", p=P), ("conv", i, 4 * u + 3))
            turns.take(1, "G", i)
            for nh in range(2):
                for tt in range(TT):
                    turns.take(tt, "gate", i, tt, nh)
                u = 6 + nh
                unit(win[:, u * 512:(u + 1) * 512].rearrange("(k p) n -> p k n", p=P), ("gate", i, TT - 1, nh))
            for tt in range(TT):
                for hg in range(2):
                    turns.take(hg, "GB", i, tt, hg)
                for hg in range(2):
                    turns.take(2 + hg, "kk", i, tt, hg)
                    turns.take(4 + hg, "qk", i, tt, hg)
                for hg in range(2):
                    turns.take(6, "Ktok", i, tt, hg)
                    turns.take(7, "Vtok", i, tt, hg)
                for hg in range(2):
                    turns.take(hg, "T0", i, tt, hg)
                for lv in range(1, LEVELS):
                    for hg in range(2):
                        turns.take(hg, "Y", i, tt, lv, hg)
                    for hg in range(2):
                        turns.take(2 + hg, "TT", i, tt, lv, hg)
                        if lv < LEVELS - 1:
                            turns.take(4 + hg, "T", i, tt, lv, hg)
                for hg in range(2):
                    turns.take(6 + hg, "W", i, tt, hg)
                for c in range(2):
                    for hg in range(2):
                        turns.take(hg, "vn", i, tt, c, hg)
                    for hg in range(2):
                        if (tt, c) != (TT - 1, 1):
                            turns.take(4 + hg, "su", i, tt, c, hg)
                for hg in range(2):
                    turns.take(2 + hg, "o", i, tt, hg)
            heads_out(i, w["a_w_out"][j])
        elif kind == 1:
            win = w["b_w_in"][j]
            for u in range(4):
                for c in range(4 * u, 4 * u + 4):
                    turns.take(c % 4, "qkT", i, c)
                    if 4 <= c < 10:
                        turns.take(4 + c % 4, "flip", i, c - 4)
                unit(win[:, u * 512:(u + 1) * 512].rearrange("(k p) n -> p k n", p=P), ("qkT", i, 4 * u + 3))
            for nh in range(2):
                for tt in range(TT):
                    turns.take(4 + 2 * nh + tt, "v", i, tt, nh)
                u = 4 + nh
                unit(win[:, u * 512:(u + 1) * 512].rearrange("(k p) n -> p k n", p=P), ("v", i, TT - 1, nh))
            for h in range(HEADS + 2):
                if h < HEADS:
                    for m in range(2):
                        turns.take(2 * (h % 2) + m, "lg", i, h, m)
                if h >= 1 and h <= HEADS:
                    turns.take(4 + (h - 1) % 2, "pT", i, h - 1)
                if h >= 2:
                    turns.take(6 + (h - 2) % 2, "ob", i, h - 2)
            heads_out(i, w["b_w_out"][j])
        else:
            win, wout = w["c_w_in"][j], w["c_w_out"][j]
            for g in range(2):
                turns.take(g, "wsT", i, g)
            for u in (4, 5, 6, 7, 0, 1, 2, 3):
                for tt in range(TT):
                    turns.take(2 + (2 * u + tt) % 4, "z", i, u, tt)
                unit(win[:, u * 512:(u + 1) * 512].rearrange("(k p) n -> p k n", p=P), ("z", i, u, TT - 1))
            for tt in range(TT):
                for g in range(4):
                    turns.take(g, "mix", i, tt, g)
            for g in range(8):
                turns.take(g % 4, "uT", i, g)
            for nh in range(2):
                for tt in range(TT):
                    turns.take(4 + 2 * tt + nh, "y", i, tt, nh)
                for kh in range(2):
                    unit(wout[kh * 1024:(kh + 1) * 1024, nh * 512:(nh + 1) * 512].rearrange("(k p) n -> p k n", p=P),
                         ("y", i, TT - 1, nh))
        for k in range(KC):
            turns.take(k, "ht", 2 * i + 1, k)
        if with_moe:
            turns.take(0, "rt", i)
            turns.loop(("moe", i), 2, E // 2)
            units.append(("moe", i))
        if i < len(kinds) - 1:
            for k in range(KC):
                turns.take(k, "ht", 2 * i + 2, k)
    return turns.at, units


def trunk(nc, w, out, kinds=ALL_KINDS, with_moe=True):
    at, units = plan(kinds, with_moe, w)
    n_layers = len(kinds)
    with ExitStack() as ctx:
        def sb(name, shape):
            return ctx.enter_context(nc.sbuf_tensor(name, shape, F32))

        def sem(name):
            return ctx.enter_context(nc.semaphore(name))

        ring = [sb(f"ring{s}", [P, 8, 512]) for s in range(SLOTS)]
        H = sb("H", [P, TT, D])
        HT = sb("HT", [P, KC, SEQ])
        gB = sb("gB", [P, D])
        bB = sb("bB", [P, D])
        K_ = sb("consts_sb", [P, C_SB])
        ident = K_[:, C_ID:C_ID + P]
        neg_mask = K_[:, C_NEG:C_NEG + P]
        cum = K_[:, C_CUM:C_CUM + P]
        blk = K_[:, C_BLK:C_BLK + P]
        tri = K_[:, C_TRI:C_TRI + P]
        onehot = bB[0:REL_BUCKETS + 1, 0:TOEP]
        work = sb("work", [P, 18432])
        lnrows = gB[:, 0:P]
        lncols = sb("lncols", [P, P])
        convrows = gB[0:96, P:3 * P].rearrange("p (a b) -> p a b", a=2)
        bsrow = gB[0:HEADS, 3 * P:4 * P]
        relrow = gB[0:HEADS, 4 * P:4 * P + TOEP]
        convcols = sb("convcols", [P, 2, 96])
        ones = sb("ones", [P, P])
        wab = sb("wab", [P, 2, KC, 16])
        alog = sb("alog", [P, 2, HEADS])
        dtb = sb("dtb", [P, 2, HEADS])
        angb = sb("angb", [P, 2, P])
        lamb = sb("lamb", [P, 4, 64])
        bngb = sb("bngb", [P, P])
        rel33 = sb("rel33", [REL_BUCKETS + 1, HEADS])
        bscol = sb("bscol", [P, HEADS])
        wr = sb("wr", [P, KC, E])
        rbias = sb("rbias", [P, E])
        epsc = sb("epsc", [P, 2])
        stats = sb("stats", [P, TT, 24])
        mv = sb("mv", [P, TT, 2])
        rs = sb("rs", [P, 4, TT])
        rt = sb("rt", [P, 8, TT * E])
        rg = sb("rg", [P, 8, TT * GROUPS])
        gates = sb("gates", [P, TT, E])
        abr = sb("abr", [P, 8, TT, HEADS])
        gsc = sb("gsc", [P, 8, TT, HEADS])
        egl = sb("egl", [P, HEADS, 2])
        ssq = sb("ssq", [P, 4, TT, HEADS])
        lm = sb("lm", [P, 8])
        sm = sb("sm", [P, HEADS, 8])

        def view(lo, a, b):
            return work[:, lo:lo + a * b].rearrange("p (a b) -> p a b", a=a)

        qT, kT, vT = view(0, HEADS, SEQ), view(2048, HEADS, SEQ), view(4096, HEADS, SEQ)
        gate = view(6144, TT, D)
        Ktok, Vtok = view(8192, HEADS, P), view(9216, HEADS, P)
        AT, attnT = view(10240, HEADS, P), view(11264, HEADS, P)
        T, Ti = view(12288, HEADS, P), view(13312, HEADS, P)
        Y, S = view(14336, HEADS, P), view(15360, HEADS, P)
        AM, DT = view(16384, HEADS, P), view(17408, HEADS, P)
        NWT, kd, kG, vnew, EGB = T, Y, AM, DT, Y
        cv = [work[:, 12288 + 256 * n:12544 + 256 * n] for n in range(4)]
        sq = [work[:, 13312 + 512 * n:13824 + 512 * n] for n in range(2)]
        lnr = [work[:, 14336 + 512 * n:14848 + 512 * n] for n in range(2)]
        O = vT
        OT = kT
        TB = work[:, 8192:8192 + HEADS * TOEP].rearrange("p (h k) -> p h k", h=HEADS)
        TBr = work[:, 15360:18432]
        flip = work[:, 11264:11392]
        L = [work[:, 11264 + 768 * n:11264 + 768 * n + 768].rearrange("p (m k) -> p m k", m=2) for n in range(2)]
        PA = [work[:, 12800 + 384 * n:12800 + 384 * n + 384] for n in range(2)]
        PT = [work[:, 13568 + 384 * n:13568 + 384 * n + 384] for n in range(2)]
        bO = view(14336, HEADS, SEQ)
        Vb = view(6144, TT, D)
        bOT = view(4096, HEADS, SEQ)
        u_ = view(0, TT, 2048)
        v_ = view(4096, TT, 2048)
        gC, bC = work[:, 8192:10240], work[:, 10240:12288]
        ws = view(12288, HEADS, P)
        wsT = view(13312, HEADS, P)
        uT = view(4096, 16, SEQ)
        hT = [view(14336 + 1024 * n, 4, SEQ) for n in range(2)]
        sil = [work[:, 16384 + 256 * n:16640 + 256 * n] for n in range(2)]

        bank = [ctx.enter_context(nc.psum_tensor(f"bank{b}", [P, 512], F32)) for b in range(8)]
        filled = [sem(f"filled{b}") for b in range(8)]
        drained = [sem(f"drained{b}") for b in range(8)]
        slot_in = [sem(f"slot_in{s}") for s in range(SLOTS)]
        params_in = sem("params_in")
        cols_ready = sem("cols_ready")
        x_ready = sem("x_ready")
        rows_in = sem("rows_in")
        rel_out = sem("rel_out")
        toep_in = sem("toep_in")
        cpar_in = sem("cpar_in")
        consts_set = sem("consts_set")
        var_ready = sem("var_ready")
        rstd_ready = sem("rstd_ready")
        xhat_ready = sem("xhat_ready")
        h_ready = sem("h_ready")
        mixed_in = sem("mixed_in")
        route_exp = sem("route_exp")
        gates_ready = sem("gates_ready")
        silu_h = sem("silu_h")
        tap_ready = sem("tap_ready")
        silu_qkv = sem("silu_qkv")
        squares = sem("squares")
        rnorm = sem("rnorm")
        qk_normed = sem("qk_normed")
        ab_exp = sem("ab_exp")
        ab_mid = sem("ab_mid")
        g_ready = sem("g_ready")
        gcol_ready = sem("gcol_ready")
        gexp = sem("gexp")
        gate_silu = sem("gate_silu")
        gate_ready = sem("gate_ready")
        egb_ready = sem("egb_ready")
        decay = sem("decay")
        qdec = sem("qdec")
        a_ready = sem("a_ready")
        masked = sem("masked")
        inv_done = sem("inv_done")
        kscaled = sem("kscaled")
        s_scaled = sem("s_scaled")
        ss_ready = sem("ss_ready")
        rms_ready = sem("rms_ready")
        o_ready = sem("o_ready")
        lam_dot = sem("lam_dot")
        lam_exp = sem("lam_exp")
        nmax = sem("nmax")
        probs = sem("probs")
        pa_ready = sem("pa_ready")
        v_ln = sem("v_ln")
        u_ready = sem("u_ready")
        v_gelu = sem("v_gelu")
        out_done = sem("out_done")
        v_chain = sem("v_chain")
        a_chain = sem("a_chain")
        p_chain = sem("p_chain")

        class Chain:

            def __init__(self, eng, s):
                self.eng, self.s, self.n = eng, s, 0

            def then(self, ins):
                ins.then_inc(self.s, 1)
                self.n += 1

            def wait(self):
                self.eng.wait_ge(self.s, self.n)

            def link(self, ins):
                self.then(ins)
                self.wait()

        def wait_data(eng, *key):
            b, n = at[key]
            eng.wait_ge(filled[b], n + 1)
            return bank[b]

        def wait_copy(eng, *key):
            b, n = at[key]
            eng.wait_ge(drained[b], n + 1)

        def emptied(ins, *key):
            ins.then_inc(drained[at[key][0]], 1)

        scratch = nc.dram_tensor("toeplitz_rows", [HEADS, TOEP], F32, kind="Internal").ap()
        lnp = {1: ("ln_mix_g", "ln_mix_b"), 0: ("ln_ffn_g", "ln_ffn_b")}
        block = ctx.enter_context(nc.Block())

        @block.sync
        def _(sp):
            def load(s, src):
                sp.dma_start(ring[s][:, :, :] if len(src.shape) == 3 and src.shape[1] == 8
                             else ring[s][:, :, :].rearrange("p a b -> p (a b)").rearrange("p (m n) -> p m n", m=4), src).then_inc(slot_in[s], 16)

            def expert_src(i, e, part):
                if part == 2:
                    return w["e_w2"][i, e].rearrange("(m p) n -> p m n", p=P)
                return w["e_w1" if part == 0 else "e_w3"][i, e].rearrange("(k p) n -> p k n", p=P)

            def release(last, back=0):
                if last[0] == "moe":
                    _, i, j, part = last
                    b = 7 if part == 2 else 3
                    sp.wait_ge(filled[b], at[("moe", i)][b] + 2 * (E // 2 - 1) + j + 1)
                else:
                    b, n = at[last]
                    sp.wait_ge(filled[b], n + 1)

            n = 0
            held = []
            for src, last in units:
                if n == 1:
                    sp.wait_ge(params_in, N_PARAMS)
                if isinstance(src, str):
                    i = last
                    for j in range(2):
                        for part in range(3):
                            if n >= SLOTS:
                                release(held[n - SLOTS])
                            load(n % SLOTS, expert_src(i, j, part))
                            held.append(("moe", i, j, part))
                            n += 1
                    first = at[("moe", i)]
                    with sp.Fori(1, E // 2) as it:
                        for j in range(2):
                            for part in range(3):
                                b = 7 if part == 2 else 3
                                sp.wait_ge(filled[b], it * 2 + (first[b] - 2 + j + 1))
                                load((n + 3 * j + part) % SLOTS, expert_src(i, it * 2 + j, part))
                    held += [("moe", i, j, part) for _ in range(E // 2 - 1) for j in range(2) for part in range(3)]
                    n += 6 * (E // 2 - 1)
                    continue
                if n >= SLOTS:
                    release(held[n - SLOTS])
                load(n % SLOTS, src)
                held.append(last)
                n += 1
            for tt in range(TT):
                sp.wait_ge(h_ready, 2 * (2 * n_layers - (0 if with_moe else n_layers)) + tt + 1)
                sp.dma_start(out[0, tt * P:(tt + 1) * P, :], H[:, tt, :]).then_inc(out_done, 16)
            sp.wait_ge(out_done, 16 * TT)

        phases = []
        for i in range(n_layers):
            phases.append((2 * i + 1, 1, i))
            if with_moe:
                phases.append((2 * i + 2, 0, i))
        last_phase = phases[-1][0]

        def bcast(src, n):
            return bass.AP(tensor=src.tensor, offset=src.offset, ap=[[0, P], [1, n]])

        @block.gpsimd
        def _(pool):
            own = Chain(pool, p_chain)
            pool.memset(rel33[:, :], -BIG).then_inc(consts_set, 1)
            pool.memset(ones[:, :], 1.0).then_inc(consts_set, 1)
            pool.memset(epsc[:, 0:1], EPS).then_inc(consts_set, 1)
            pool.memset(epsc[:, 1:2], L2EPS).then_inc(consts_set, 1)
            pool.wait_ge(x_ready, 16)
            for k in range(KC):
                wait_data(pool, "ht", 0, k)
            for tt in range(TT):
                pool.tensor_scalar(H[:, tt, :], H[:, tt, :], ALPHA, None, ALU.mult).then_inc(h_ready, 1)

            ph = 0

            def residual(phase, which, i):
                nonlocal ph
                g, b = lnp[which]
                if ph:
                    own.wait()
                else:
                    wait_data(pool, "cols")
                    pool.wait_ge(rel_out, 16)
                pool.dma_start(gB[:, :], bcast(w[g][i], D)).then_inc(rows_in, 16)
                pool.dma_start(bB[:, :], bcast(w[b][i], D)).then_inc(rows_in, 16)
                ph += 1
                pool.wait_ge(rows_in, 32 * ph)
                if phase != last_phase:
                    for k in range(KC):
                        wait_data(pool, "ht", phase, k)
                else:
                    pool.wait_ge(xhat_ready, 2 * ph)
                for tt in range(TT):
                    own.then(pool.tensor_tensor(H[:, tt, :], H[:, tt, :], gB[:, :], ALU.mult))
                own.wait()
                for tt in range(TT):
                    ins = pool.tensor_tensor(H[:, tt, :], H[:, tt, :], bB[:, :], ALU.add)
                    if phase == last_phase:
                        ins.then_inc(h_ready, 1)
                    else:
                        own.then(ins)
                if phase != last_phase:
                    own.wait()
                    for tt in range(TT):
                        pool.tensor_scalar(H[:, tt, :], H[:, tt, :], ALPHA, None, ALU.mult).then_inc(h_ready, 1)

            def delta(i, j):
                for n in range(8):
                    src = (qT if n < 4 else kT)[:, 2 * (n % 4):2 * (n % 4) + 2, :]
                    pool.wait_ge(silu_qkv, 18 * j + 2 * n + 2)
                    if n >= 2:
                        wait_data(pool, "ss", i, n - 2)
                    pool.tensor_tensor(sq[n % 2].rearrange("p (a b) -> p a b", a=2), src, src, ALU.mult).then_inc(squares, 1)
                pool.wait_ge(gate_silu, j + 1)
                for tt in range(TT):
                    gt = gate[:, tt, :].rearrange("p (h d) -> p h d", h=HEADS)
                    pool.tensor_tensor(gt, gt, angb[:, j, :].unsqueeze(1).to_broadcast([P, HEADS, P]), ALU.mult).then_inc(gate_ready, 1)
                for tt in range(TT):
                    for hg in range(2):
                        pool.wait_ge(egb_ready, 4 * j + 2 * tt + hg + 1)
                        wait_data(pool, "qk", i, tt, hg)
                        sl = qT[:, 4 * hg:4 * hg + 4, tt * P:(tt + 1) * P]
                        pool.tensor_tensor(sl, sl, EGB[:, 4 * hg:4 * hg + 4, :], ALU.mult).then_inc(qdec, 1)

            pool.wait_ge(params_in, N_PARAMS)
            for i, kind in enumerate(kinds):
                j = kinds[:i].count(kind)
                if kind == 0:
                    delta(i, j)
                residual(2 * i + 1, 1, i)
                if with_moe:
                    residual(2 * i + 2, 0, i)

        @block.scalar
        def _(act):
            own = Chain(act, a_chain)
            a = nc.scalar.activation
            act.dma_start(H[:, :, :], w["x"][0].rearrange("(t p) d -> p t d", p=P)).then_inc(x_ready, 16)
            small = [(K_[:, :], w["consts"][:, 0:C_SB]), (onehot, w["consts"][0:REL_BUCKETS + 1, C_OH:C_FLIP])]
            for n, name in enumerate(("ln_mix_g", "ln_mix_b", "ln_ffn_g", "ln_ffn_b")):
                small.append((lnrows[32 * n:32 * n + 32, :], w[name].rearrange("l (k p) -> (l k) p", p=P)))
            for j in range(2):
                small.append((convrows[:, j, :], w["a_conv"][j].rearrange("t (c p) -> (t c) p", p=P)))
                small.append((wab[:, j, :, :], w["a_w_in"][j][:, 4096:4112].rearrange("(k p) n -> p k n", p=P)))
                small.append((alog[:, j, :], bcast(w["a_a_log"][j], HEADS)))
                small.append((dtb[:, j, :], bcast(w["a_dt_bias"][j], HEADS)))
                small.append((angb[:, j, :], bcast(w["a_norm_g"][j], P)))
            small.append((lamb[:, :, :].rearrange("p a b -> p (a b)"), bcast(w["b_lambda"], 256)))
            small.append((bngb[:, :], bcast(w["b_norm_g"], P)))
            small.append((bsrow[:, :], w["c_b_s"][0]))
            small.append((wr[:, :, :], w["w_router"].rearrange("(k p) n -> p k n", p=P)))
            small.append((rbias[:, :], bcast(w["router_bias"], E)))
            assert 16 * (len(small) + 1) == N_PARAMS
            for dst, src in small:
                act.dma_start(dst, src).then_inc(params_in, 16)
            act.wait_ge(consts_set, 4)
            act.dma_start(rel33[0:REL_BUCKETS, :], w["rel_bias"]).then_inc(params_in, 16)
            act.wait_ge(params_in, N_PARAMS)
            emptied(a(relrow[:, :], wait_data(act, "relrow")[0:HEADS, 0:TOEP], ACT.Copy), "relrow")
            wait_copy(act, "relrow")
            act.dma_start(scratch, relrow[:, :]).then_inc(rel_out, 16)

            def ht_chunks(phase):
                for k in range(0, KC, 2):
                    ps = wait_data(act, "ht", phase, k)
                    if phase == 0:
                        emptied(a(HT[:, k, :], ps[:, 0:SEQ], ACT.Copy), "ht", phase, k)
                    else:
                        c = (0 if phase % 2 else 2) * 32 + (phase - 1) // 2 * 8 + k
                        emptied(a(HT[:, k, :], ps[:, 0:SEQ], ACT.Identity, scale=lncols[:, c:c + 1],
                                  bias=lncols[:, c + 32:c + 33]), "ht", phase, k)

            ln_count = 0

            def rsqrt(dst, src, eps_col, count):
                own.link(a(dst, src, ACT.Ln, bias=epsc[:, eps_col:eps_col + 1]))
                a(dst, dst, ACT.Exp, scale=-0.5).then_inc(rstd_ready, 1)

            rsq = 0

            def ln_rstd():
                nonlocal rsq
                rsq += 1
                act.wait_ge(var_ready, rsq)
                rsqrt(rs[:, 0, :], mv[:, :, 1], 0, rsq)

            def heads_norm(nn):
                act.wait_ge(ss_ready, nn + 1)
                own.link(a(ssq[:, 1, :, :], ssq[:, 0, :, :], ACT.Ln, bias=epsc[:, 0:1], scale=1.0 / P))
                a(ssq[:, 2, :, :], ssq[:, 1, :, :], ACT.Exp, scale=-0.5).then_inc(rms_ready, 1)

            def heads_out_T(i, nn, dst):
                for g in range(0, 4, 2):
                    ps = wait_data(act, "oT", i, g)
                    emptied(a(dst[:, 2 * g:2 * g + 2, :], ps[:, :].rearrange("p (a b) -> p a b", a=2), ACT.Copy), "oT", i, g)

            def delta(i, j):
                emptied(a(abr[:, 0:2, :, :].rearrange("p k t h -> p t k h"),
                          wait_data(act, "ab", i)[:, 0:32].rearrange("p (t k h) -> p t k h", t=TT, k=2), ACT.Copy), "ab", i)
                act.wait_ge(ab_mid, 2 * j + 1)
                own.link(a(abr[:, 4, :, :], abr[:, 3, :, :], ACT.Exp, scale=-1.0))
                own.then(a(abr[:, 5, :, :], abr[:, 1, :, :], ACT.Exp, scale=-1.0))
                own.then(a(abr[:, 4, :, :], abr[:, 4, :, :], ACT.Ln, bias=1.0))
                a(gsc[:, 7, 0, :], alog[:, j, :], ACT.Exp).then_inc(ab_exp, 1)

                def silu(c):
                    wait_copy(act, "conv", i, c)
                    dst = (qT, kT)[c // 8][:, c % 8, :]
                    a(dst, cv[c % 4], ACT.Silu).then_inc(silu_qkv, 1)

                def tap(c):
                    ps = wait_data(act, "conv", i, c)
                    if c < 16:
                        if c >= 4:
                            act.wait_ge(silu_qkv, 18 * j + c - 3)
                        dst = cv[c % 4]
                    else:
                        dst = vT[:, c - 16, :]
                    a(dst, ps[:, 0:SEQ], ACT.Copy, scale=convcols[:, j, 72 + c:73 + c]).then_inc(tap_ready, 1)

                for c in range(17):
                    tap(c) if c < 16 else None
                    if c >= 1:
                        silu(c - 1)
                for c in range(16, 24):
                    tap(c)
                    n = c - 16
                    ps = wait_data(act, "ss", i, n)
                    if n >= 2:
                        act.wait_ge(qk_normed, 8 * j + n - 1)
                    emptied(a(lnr[n % 2], ps[:, :], ACT.Ln, bias=epsc[:, 1:2]), "ss", i, n)
                    wait_copy(act, "ss", i, n)
                    a(lnr[n % 2], lnr[n % 2], ACT.Exp, scale=-0.5).then_inc(rnorm, 1)
                for nh in range(2):
                    for tt in range(TT):
                        emptied(a(gate[:, tt, nh * 512:(nh + 1) * 512], wait_data(act, "gate", i, tt, nh)[:, :], ACT.Copy), "gate", i, tt, nh)
                for c in range(16, 24):
                    wait_copy(act, "conv", i, c)
                for n in range(2):
                    a(vT[:, 4 * n:4 * n + 4, :], vT[:, 4 * n:4 * n + 4, :], ACT.Silu).then_inc(silu_qkv, 1)
                for nh in range(2):
                    for tt in range(TT):
                        wait_copy(act, "gate", i, tt, nh)
                a(gate[:, :, :], gate[:, :, :], ACT.Silu).then_inc(gate_silu, 1)
                act.wait_ge(gcol_ready, j + 1)
                own.then(a(gsc[:, 4, :, :], gsc[:, 0, :, :], ACT.Exp))
                a(gsc[:, 5, :, :], gsc[:, 3, :, :], ACT.Exp).then_inc(gexp, 1)
                for tt in range(TT):
                    for hg in range(2):
                        ps = wait_data(act, "GB", i, tt, hg)
                        if tt:
                            wait_data(act, "su", i, 0, 1, hg)
                        a(EGB[:, 4 * hg:4 * hg + 4, :], ps[:, :].rearrange("p (a b) -> p a b", a=4), ACT.Exp).then_inc(egb_ready, 1)
                    for hg in range(2):
                        wait_copy(act, "GB", i, tt, hg)
                        for h in range(4 * hg, 4 * hg + 4):
                            ins = a(DT[:, h, :], DT[:, h, :], ACT.Exp, bias=gsc[:, 2, tt, h:h + 1])
                        ins.then_inc(decay, 1)
                    for hg in range(2):
                        for key, dst in (("Ktok", Ktok), ("Vtok", Vtok)):
                            ps = wait_data(act, key, i, tt, hg)
                            if tt and key == "Vtok":
                                wait_data(act, "vn", i, 0, 0, hg)
                            emptied(a(dst[:, 4 * hg:4 * hg + 4, :], ps[:, :].rearrange("p (a b) -> p a b", a=4), ACT.Copy), key, i, tt, hg)
                    for hg in range(2):
                        ps = wait_data(act, "T0", i, tt, hg)
                        if tt:
                            wait_data(act, "vn", i, 0, 1, hg)
                        emptied(a(T[:, 4 * hg:4 * hg + 4, :], ps[:, :].rearrange("p (a b) -> p a b", a=4), ACT.Copy), "T0", i, tt, hg)
                    for lv in range(1, LEVELS):
                        for hg in range(2):
                            ps = wait_data(act, "Y", i, tt, lv, hg)
                            if lv == 1:
                                act.wait_ge(qdec, 4 * j + 2 * tt + hg + 1)
                            else:
                                wait_data(act, "T", i, tt, lv - 1, hg)
                            emptied(a(Y[:, 4 * hg:4 * hg + 4, :], ps[:, :].rearrange("p (a b) -> p a b", a=4), ACT.Copy), "Y", i, tt, lv, hg)
                    for hg in range(2):
                        wait_data(act, "TT", i, tt, LEVELS - 1, hg)
                        for h in range(4 * hg, 4 * hg + 4):
                            a(kG[:, h, :], Ktok[:, h, :], ACT.Copy, scale=gsc[:, 4, tt, h:h + 1])
                            ins = a(kd[:, h, :], Ktok[:, h, :], ACT.Copy, scale=gsc[:, 5, tt, h:h + 1])
                        ins.then_inc(kscaled, 1)
                    for hg in range(2):
                        ps = wait_data(act, "W", i, tt, hg)
                        emptied(a(NWT[:, 4 * hg:4 * hg + 4, :], ps[:, :].rearrange("p (a b) -> p a b", a=4), ACT.Copy, scale=-1.0), "W", i, tt, hg)
                    for hg in range(2):
                        ps = wait_data(act, "o", i, tt, hg)
                        emptied(a(O[:, 4 * hg:4 * hg + 4, tt * P:(tt + 1) * P], ps[:, :].rearrange("p (a b) -> p a b", a=4), ACT.Copy), "o", i, tt, hg)

            def attention(i, j):
                if j == 0:
                    act.wait_ge(lam_dot, 1)
                    a(lm[:, 2:4], lm[:, 0:2], ACT.Exp).then_inc(lam_exp, 1)
                act.wait_ge(rel_out, 16)
                for k in range(KC):
                    wait_data(act, "ht", 2 * i, k)
                act.dma_start(flip, w["consts"][:, C_FLIP:C_ALL]).then_inc(toep_in, 16)
                for lo, n, off in ((0, P, P), (P, SEQ, 0)):
                    act.dma_start(TBr.rearrange("p (h k) -> p h k", h=HEADS)[:, :, lo:lo + n],
                                  bass.AP(tensor=scratch.tensor, offset=off, ap=[[1, P], [TOEP, HEADS], [1, n]])).then_inc(toep_in, 16)
                for c in range(16):
                    ps = wait_data(act, "qkT", i, c)
                    emptied(a((qT, kT)[c // 8][:, c % 8, :], ps[:, 0:SEQ], ACT.Copy, scale=0.125 if c < 8 else 1.0), "qkT", i, c)
                for nh in range(2):
                    for tt in range(TT):
                        emptied(a(Vb[:, tt, nh * 512:(nh + 1) * 512], wait_data(act, "v", i, tt, nh)[:, :], ACT.Copy), "v", i, tt, nh)
                for h in range(HEADS + 2):
                    if h < HEADS:
                        act.wait_ge(nmax, HEADS * j + h + 1)
                        for m in range(2):
                            a(L[h % 2][:, m, 0:P], L[h % 2][:, m, 0:P], ACT.Exp, bias=sm[:, h, m:m + 1], accum_out=sm[:, h, 4 + m:5 + m])
                            ins = a(L[h % 2][:, m, P:TOEP], L[h % 2][:, m, P:TOEP], ACT.Exp, bias=sm[:, h, 2 + m:3 + m], accum_out=sm[:, h, 6 + m:7 + m])
                        ins.then_inc(probs, 1)
                    if 1 <= h <= HEADS:
                        ps = wait_data(act, "pT", i, h - 1)
                        if h - 1 >= 2:
                            wait_data(act, "ob", i, h - 3)
                        emptied(a(PT[(h - 1) % 2], ps[:, 0:TOEP], ACT.Copy), "pT", i, h - 1)
                    if h >= 2:
                        g = h - 2
                        emptied(a(bO[:, g, :], wait_data(act, "ob", i, g)[:, 0:SEQ], ACT.Copy), "ob", i, g)

            def gmlp(i, j):
                for k in range(KC):
                    wait_data(act, "ht", 2 * i, k)
                act.dma_start(gC, bcast(w["c_ln_g"][j], 2048)).then_inc(cpar_in, 16)
                act.dma_start(bC, bcast(w["c_ln_b"][j], 2048)).then_inc(cpar_in, 16)
                act.dma_start(ws, w["c_w_s"][j].rearrange("g t s -> t g s")).then_inc(cpar_in, 16)
                for u in (4, 5, 6, 7, 0, 1, 2, 3):
                    for tt in range(TT):
                        ps = wait_data(act, "z", i, u, tt)
                        dst = v_[:, tt, (u - 4) * 512:(u - 3) * 512] if u >= 4 else u_[:, tt, u * 512:(u + 1) * 512]
                        emptied(a(dst, ps[:, :], ACT.Gelu), "z", i, u, tt)
                    if u == 7:
                        ln_rstd()
                for g in range(0, 8, 2):
                    ps = wait_data(act, "uT", i, g)
                    emptied(a(uT[:, 2 * g:2 * g + 2, :], ps[:, :].rearrange("p (a b) -> p a b", a=2), ACT.Copy), "uT", i, g)

            def experts(i):
                emptied(a(rt[:, 0, :], wait_data(act, "rt", i)[:, 0:TT * E], ACT.Exp, scale=-1.0), "rt", i)
                first = at[("moe", i)]
                with act.Fori(0, E // 2) as it:
                    for j in range(2):
                        for m in range(4):
                            act.wait_ge(filled[m], it * 2 + (first[m] + j + 1))
                            b, back = (m - 2, j) if m >= 2 else (m + 2, j - 1)
                            act.wait_ge(drained[b], it * 2 + (first[b] + back + 1))
                            a(sil[m % 2], bank[m][:, 0:SEQ], ACT.Silu).then_inc(silu_h, 1)

            ht_chunks(0)
            nn = 0
            for i, kind in enumerate(kinds):
                j = kinds[:i].count(kind)
                if kind == 0:
                    delta(i, j)
                    heads_norm(nn)
                    heads_out_T(i, nn, OT)
                    nn += 1
                elif kind == 1:
                    attention(i, j)
                    heads_norm(nn)
                    heads_out_T(i, nn, bOT)
                    nn += 1
                else:
                    gmlp(i, j)
                ln_rstd()
                if 2 * i + 1 != last_phase:
                    ht_chunks(2 * i + 1)
                if with_moe:
                    experts(i)
                    ln_rstd()
                if i < n_layers - 1:
                    ht_chunks(2 * i + 2)

        @block.vector
        def _(dve):
            v = nc.vector
            own = Chain(dve, v_chain)
            dve.wait_ge(params_in, N_PARAMS)
            ps = wait_data(dve, "cols")
            v.tensor_copy(lncols[:, :], ps[:, 0:P])
            v.tensor_copy(convcols[:, 0, :], ps[:, P:P + 96])
            v.tensor_copy(convcols[:, 1, :], ps[:, 256:352])
            emptied(v.tensor_copy(bscol[:, :], ps[:, 384:392]), "cols")
            wait_copy(dve, "cols")

            def ht_chunks(phase):
                for k in range(1, KC, 2):
                    ps = wait_data(dve, "ht", phase, k)
                    if phase == 0:
                        emptied(v.tensor_copy(HT[:, k, :], ps[:, 0:SEQ]), "ht", phase, k)
                    else:
                        c = (0 if phase % 2 else 2) * 32 + (phase - 1) // 2 * 8 + k
                        emptied(v.tensor_scalar(HT[:, k, :], ps[:, 0:SEQ], lncols[:, c:c + 1], lncols[:, c + 32:c + 33],
                                                ALU.mult, ALU.add), "ht", phase, k)

            rsq = 0
            lnn = 0

            def norm(X, blocks):
                nonlocal rsq
                for tt in range(TT):
                    for b in range(blocks):
                        own.then(v.bn_stats(stats[:, tt, 6 * b:6 * b + 6], X[:, tt, b * 512:(b + 1) * 512]))
                own.wait()
                for tt in range(TT):
                    ins = v.bn_aggr(mv[:, tt, :], stats[:, tt, 0:6 * blocks])
                    if tt < TT - 1:
                        own.then(ins)
                rsq += 1
                ins.then_inc(var_ready, 1)
                dve.wait_ge(rstd_ready, rsq)
                own.link(v.tensor_tensor(rs[:, 1, :], rs[:, 0, :], rs[:, 0, :], ALU.mult))
                own.link(v.scalar_tensor_tensor(rs[:, 2, :], mv[:, :, 1], EPS, rs[:, 1, :], ALU.add, ALU.mult))
                own.link(v.tensor_scalar(rs[:, 1, :], rs[:, 2, :], -0.5, 1.5, ALU.mult, ALU.add))
                own.link(v.tensor_tensor(rs[:, 3, :], rs[:, 1, :], rs[:, 0, :], ALU.mult))

            def layer_norm():
                nonlocal lnn
                norm(H, 2)
                for tt in range(TT):
                    v.tensor_scalar(H[:, tt, :], H[:, tt, :], mv[:, tt, 0:1], rs[:, 3, tt:tt + 1],
                                    ALU.subtract, ALU.mult).then_inc(xhat_ready, 1)
                lnn += 1

            def add_mixed(i):
                for nh in range(2):
                    for tt in range(TT):
                        ps = wait_data(dve, "y", i, tt, nh)
                        sl = H[:, tt, nh * 512:(nh + 1) * 512]
                        emptied(v.tensor_tensor(sl, ps[:, :], sl, ALU.add), "y", i, tt, nh)
                for nh in range(2):
                    for tt in range(TT):
                        wait_copy(dve, "y", i, tt, nh)

            def heads_norm(nn, X, gain, scale):
                for tt in range(TT):
                    own.wait()
                    own.link(v.tensor_tensor(X2, X(tt), X(tt), ALU.mult))
                    ins = v.tensor_reduce(ssq[:, 0, tt, :], X2, AX, ALU.add)
                    own.then(ins) if tt < TT - 1 else ins.then_inc(ss_ready, 1)
                dve.wait_ge(rms_ready, nn + 1)
                own.link(v.tensor_scalar(ssq[:, 3, :, :], ssq[:, 2, :, :], scale, None, ALU.mult))
                for tt in range(TT):
                    own.then(v.tensor_tensor(X(tt), X(tt), ssq[:, 3, tt, :].unsqueeze(2).to_broadcast([P, HEADS, P]), ALU.mult))
                own.wait()
                for tt in range(TT):
                    v.tensor_tensor(X(tt), X(tt), gain(tt), ALU.mult).then_inc(o_ready, 1)

            def heads_out_T(i, nn, dst):
                for g in range(1, 4, 2):
                    ps = wait_data(dve, "oT", i, g)
                    emptied(v.tensor_copy(dst[:, 2 * g:2 * g + 2, :], ps[:, :].rearrange("p (a b) -> p a b", a=2)), "oT", i, g)

            def delta(i, j):
                wait_copy(dve, "ab", i)
                own.link(v.tensor_tensor(abr[:, 2, :, :], abr[:, 0, :, :], dtb[:, j, :].unsqueeze(1).to_broadcast([P, TT, HEADS]), ALU.add))
                own.link(v.tensor_scalar(abr[:, 3, :, :], abr[:, 2, :, :], -1.0, None, ALU.mult))
                v.tensor_tensor(abr[:, 3, :, :], abr[:, 2, :, :], abr[:, 3, :, :], ALU.max).then_inc(ab_mid, 1)
                dve.wait_ge(ab_exp, j + 1)
                own.link(v.tensor_scalar(abr[:, 5, :, :], abr[:, 5, :, :], 1.0, None, ALU.add))
                own.then(v.reciprocal(gsc[:, 6, :, :], abr[:, 5, :, :]))
                own.link(v.scalar_tensor_tensor(abr[:, 6, :, :], abr[:, 2, :, :], 0.0, abr[:, 4, :, :], ALU.max, ALU.add))
                own.link(v.tensor_scalar(abr[:, 6, :, :], abr[:, 6, :, :], -1.0, None, ALU.mult))
                v.tensor_tensor(abr[:, 7, :, :], abr[:, 6, :, :], gsc[:, 7, 0, :].unsqueeze(1).to_broadcast([P, TT, HEADS]), ALU.mult).then_inc(ab_mid, 1)

                def conv(c):
                    ps = wait_data(dve, "conv", i, c)
                    dve.wait_ge(tap_ready, 24 * j + c + 1)
                    dst = cv[c % 4] if c < 16 else vT[:, c - 16, :]
                    for back in (1, 2, 3):
                        col = 24 * (3 - back) + c
                        ins = v.scalar_tensor_tensor(dst[:, back:SEQ], ps[:, 0:SEQ - back], convcols[:, j, col:col + 1],
                                                     dst[:, back:SEQ], ALU.mult, ALU.add)
                        if back < 3:
                            own.link(ins)
                    emptied(ins, "conv", i, c)

                def normed(n):
                    dve.wait_ge(rnorm, 8 * j + n + 1)
                    dst = (qT if n < 4 else kT)[:, 2 * (n % 4):2 * (n % 4) + 2, :]
                    sc = float(P) ** -0.5 if n < 4 else 1.0
                    v.scalar_tensor_tensor(dst, dst, sc, lnr[n % 2].rearrange("p (a b) -> p a b", a=2), ALU.mult, ALU.mult).then_inc(qk_normed, 1)

                for c in range(24):
                    conv(c)
                    if c >= 17:
                        normed(c - 17)
                normed(7)
                ps = wait_data(dve, "G", i)
                own.then(v.tensor_copy(gsc[:, 0:2, :, :], ps[:, 0:32].rearrange("p (k t h) -> p k t h", k=2, t=TT)))
                own.wait()
                emptied(v.tensor_scalar(gsc[:, 2, :, :], ps[:, 0:16].rearrange("p (t h) -> p t h", t=TT), -1.0, None, ALU.mult), "G", i)
                v.tensor_tensor(gsc[:, 3, :, :], gsc[:, 1, :, :], gsc[:, 0, :, :], ALU.subtract).then_inc(gcol_ready, 1)
                own.then(v.memset(S[:, :, :], 0.0))
                for tt in range(TT):
                    for hg in range(2):
                        hs = slice(4 * hg, 4 * hg + 4)
                        ps = wait_data(dve, "GB", i, tt, hg)
                        dve.wait_ge(egb_ready, 4 * j + 2 * tt + hg + 1)
                        if tt:
                            wait_data(dve, "o", i, 0, hg)
                        g4 = ps[:, :].rearrange("p (a b) -> p a b", a=4)
                        own.then(v.tensor_tensor(DT[:, hs, :], g4, neg_mask.unsqueeze(1).to_broadcast([P, 4, P]), ALU.add))
                        own.wait()
                        if hg == 0 and tt:
                            dve.wait_ge(s_scaled, 6 * j + 4)
                        emptied(v.tensor_copy(egl[:, hs, :], EGB[:, hs, 63:128:64]), "GB", i, tt, hg)
                    for hg in range(2):
                        hs = slice(4 * hg, 4 * hg + 4)
                        dve.wait_ge(decay, 4 * j + 2 * tt + hg + 1)
                        ps = wait_data(dve, "kk", i, tt, hg)
                        for h in range(4 * hg, 4 * hg + 4):
                            ins = v.scalar_tensor_tensor(AT[:, h, :], ps[:, (h % 4) * P:(h % 4 + 1) * P], gsc[:, 6, tt, h:h + 1],
                                                         DT[:, h, :], ALU.mult, ALU.mult)
                        emptied(ins, "kk", i, tt, hg)
                        ps = wait_data(dve, "qk", i, tt, hg)
                        if tt:
                            wait_data(dve, "o", i, 0, hg)
                        emptied(v.tensor_tensor(attnT[:, hs, :], ps[:, :].rearrange("p (a b) -> p a b", a=4), DT[:, hs, :], ALU.mult), "qk", i, tt, hg)
                    for hg in range(2):
                        hs = slice(4 * hg, 4 * hg + 4)
                        wait_copy(dve, "kk", i, tt, hg)
                        if tt:
                            wait_data(dve, "vn", i, 0, 1, hg)
                            wait_data(dve, "W", i, 0, hg)
                        own.link(v.tensor_tensor(AM[:, hs, :], AT[:, hs, :], level(0).unsqueeze(1).to_broadcast([P, 4, P]), ALU.mult))
                        v.scalar_tensor_tensor(Ti[:, hs, :], AM[:, hs, :], -1.0, ident.unsqueeze(1).to_broadcast([P, 4, P]),
                                               ALU.mult, ALU.add).then_inc(inv_done, 1)
                    for lv in range(1, LEVELS):
                        for hg in range(2):
                            hs = slice(4 * hg, 4 * hg + 4)
                            if lv == 1:
                                dve.wait_ge(inv_done, 4 * j + 2 * tt + hg + 1)
                            else:
                                wait_data(dve, "Y", i, tt, lv - 1, hg)
                            v.tensor_tensor(AM[:, hs, :], AT[:, hs, :], level(lv).unsqueeze(1).to_broadcast([P, 4, P]), ALU.mult).then_inc(masked, 1)
                        for hg in range(2):
                            hs = slice(4 * hg, 4 * hg + 4)
                            psT = wait_data(dve, "TT", i, tt, lv, hg)
                            if lv < LEVELS - 1:
                                psU = wait_data(dve, "T", i, tt, lv, hg)
                            if lv > 1:
                                wait_copy(dve, "TT", i, tt, lv - 1, hg)
                                wait_copy(dve, "T", i, tt, lv - 1, hg)
                            emptied(v.tensor_tensor(Ti[:, hs, :], Ti[:, hs, :], psT[:, :].rearrange("p (a b) -> p a b", a=4), ALU.subtract), "TT", i, tt, lv, hg)
                            if lv < LEVELS - 1:
                                emptied(v.tensor_tensor(T[:, hs, :], T[:, hs, :], psU[:, :].rearrange("p (a b) -> p a b", a=4), ALU.subtract), "T", i, tt, lv, hg)
                    for c in range(2):
                        r0 = slice(64 * c, 64 * c + 64)
                        last = (tt, c) == (TT - 1, 1)
                        for hg in range(2):
                            hs = slice(4 * hg, 4 * hg + 4)
                            ps = wait_data(dve, "vn", i, tt, c, hg)
                            emptied(v.tensor_tensor(vnew[r0, hs, :], ps[r0, :].rearrange("p (a b) -> p a b", a=4),
                                                    gsc[r0, 6, tt, hs].unsqueeze(2).to_broadcast([64, 4, P]), ALU.mult), "vn", i, tt, c, hg)
                            if not last:
                                v.tensor_tensor(S[:, hs, :], S[:, hs, :], egl[:, hs, c:c + 1].to_broadcast([P, 4, P]), ALU.mult).then_inc(s_scaled, 1)
                        if last:
                            continue
                        for hg in range(2):
                            hs = slice(4 * hg, 4 * hg + 4)
                            ps = wait_data(dve, "su", i, tt, c, hg)[:, :].rearrange("p (a b) -> p a b", a=4)
                            dve.wait_ge(s_scaled, 6 * j + 2 * (2 * tt + c) + hg + 1)
                            emptied(v.tensor_tensor(S[:, hs, :], ps, S[:, hs, :], ALU.add), "su", i, tt, c, hg)
                for tt in range(TT):
                    for hg in range(2):
                        wait_copy(dve, "o", i, tt, hg)
                dve.wait_ge(gate_ready, 2 * j + 2)

            def level(lv):
                return K_[:, C_LV + lv * P:C_LV + (lv + 1) * P]

            def attention(i, j, lam_init):
                if j == 0:
                    own.link(v.tensor_tensor(lamb[:, 0:4:2, :], lamb[:, 0:4:2, :], lamb[:, 1:4:2, :], ALU.mult))
                    v.tensor_reduce(lm[:, 0:2], lamb[:, 0:4:2, :], AX, ALU.add).then_inc(lam_dot, 1)
                    dve.wait_ge(lam_exp, 1)
                    own.link(v.tensor_tensor(lm[:, 4:5], lm[:, 3:4], lm[:, 2:3], ALU.subtract))
                    own.link(v.tensor_scalar(lm[:, 5:6], lm[:, 4:5], -lam_init, None, ALU.add))
                for n in range(6):
                    ps = wait_data(dve, "flip", i, n)
                    emptied(v.tensor_copy(work[:, 8192 + n * 512:8192 + (n + 1) * 512], ps[:, :]), "flip", i, n)
                for n in range(6):
                    wait_copy(dve, "flip", i, n)
                for h in range(HEADS + 1):
                    if h < HEADS:
                        Lh = L[h % 2]
                        if h >= 2:
                            dve.wait_ge(pa_ready, HEADS * j + h - 1)
                        for m in range(2):
                            ps = wait_data(dve, "lg", i, h, m)
                            emptied(v.tensor_tensor(Lh[:, m, :], ps[:, 0:TOEP], TB[:, h, :], ALU.add), "lg", i, h, m)
                        wait_copy(dve, "lg", i, h, 0)
                        wait_copy(dve, "lg", i, h, 1)
                        own.then(v.tensor_reduce(sm[:, h, 0:2], Lh[:, :, 0:P], AX, ALU.max))
                        own.link(v.tensor_reduce(sm[:, h, 2:4], Lh[:, :, P:TOEP], AX, ALU.max))
                        v.tensor_scalar(sm[:, h, 0:4], sm[:, h, 0:4], -1.0, None, ALU.mult).then_inc(nmax, 1)
                    if h >= 1:
                        g = h - 1
                        Lg, A = L[g % 2], PA[g % 2]
                        dve.wait_ge(probs, HEADS * j + g + 1)
                        own.link(v.reciprocal(sm[:, g, 4:8], sm[:, g, 4:8]))
                        own.link(v.tensor_scalar(sm[:, g, 5:8:2], sm[:, g, 5:8:2], lm[:, 5:6], None, ALU.mult))
                        if g >= 2:
                            wait_data(dve, "pT", i, g - 2)
                        own.then(v.tensor_scalar(A[:, 0:P], Lg[:, 0, 0:P], sm[:, g, 4:5], None, ALU.mult))
                        own.link(v.tensor_scalar(A[:, P:TOEP], Lg[:, 0, P:TOEP], sm[:, g, 6:7], None, ALU.mult))
                        own.then(v.scalar_tensor_tensor(A[:, 0:P], Lg[:, 1, 0:P], sm[:, g, 5:6], A[:, 0:P], ALU.mult, ALU.add))
                        v.scalar_tensor_tensor(A[:, P:TOEP], Lg[:, 1, P:TOEP], sm[:, g, 7:8], A[:, P:TOEP], ALU.mult, ALU.add).then_inc(pa_ready, 1)
                for h in range(HEADS):
                    wait_copy(dve, "ob", i, h)

            def gmlp(i, j):
                dve.wait_ge(cpar_in, 48)
                for g in range(2):
                    ps = wait_data(dve, "wsT", i, g)
                    emptied(v.tensor_tensor(wsT[:, 4 * g:4 * g + 4, :], ps[:, :].rearrange("p (a b) -> p a b", a=4),
                                            tri.unsqueeze(1).to_broadcast([P, 4, P]), ALU.mult), "wsT", i, g)
                for u in (4, 5, 6, 7):
                    for tt in range(TT):
                        wait_copy(dve, "z", i, u, tt)
                norm(v_, 4)
                for tt in range(TT):
                    own.link(v.tensor_scalar(v_[:, tt, :], v_[:, tt, :], mv[:, tt, 0:1], rs[:, 3, tt:tt + 1], ALU.subtract, ALU.mult))
                    own.link(v.tensor_tensor(v_[:, tt, :], v_[:, tt, :], gC, ALU.mult))
                    v.tensor_tensor(v_[:, tt, :], v_[:, tt, :], bC, ALU.add).then_inc(v_ln, 1)
                for tt in range(TT):
                    for g2 in range(4):
                        wait_copy(dve, "z", i, g2, tt)
                        ps = wait_data(dve, "mix", i, tt, g2)
                        for g in (2 * g2, 2 * g2 + 1):
                            sl = u_[:, tt, g * 256:(g + 1) * 256]
                            ins = v.scalar_tensor_tensor(sl, ps[:, (g % 2) * 256:(g % 2 + 1) * 256], bscol[:, g:g + 1], sl, ALU.add, ALU.mult)
                        emptied(ins, "mix", i, tt, g2)
                for g in range(1, 8, 2):
                    ps = wait_data(dve, "uT", i, g)
                    emptied(v.tensor_copy(uT[:, 2 * g:2 * g + 2, :], ps[:, :].rearrange("p (a b) -> p a b", a=2)), "uT", i, g)

            def route(i):
                wait_copy(dve, "rt", i)
                R = [rt[:, n, :] for n in range(8)]
                V3 = lambda n: rt[:, n, :].rearrange("p (t e) -> p t e", t=TT)
                G4 = lambda n: rt[:, n, :].rearrange("p (a e) -> p a e", e=4)
                own.link(v.tensor_scalar(R[1], R[0], 1.0, None, ALU.add))
                own.link(v.reciprocal(R[1], R[1]))
                own.link(v.tensor_tensor(V3(2), V3(1), rbias[:, :].unsqueeze(1).to_broadcast([P, TT, E]), ALU.add))
                g = [rg[:, n, :] for n in range(8)]
                s = G4(2)
                own.then(v.tensor_tensor(g[0], s[:, :, 0], s[:, :, 1], ALU.max))
                own.then(v.tensor_tensor(g[1], s[:, :, 0], s[:, :, 1], ALU.min))
                own.then(v.tensor_tensor(g[2], s[:, :, 2], s[:, :, 3], ALU.max))
                own.link(v.tensor_tensor(g[3], s[:, :, 2], s[:, :, 3], ALU.min))
                own.then(v.tensor_tensor(g[4], g[0], g[2], ALU.max))
                own.then(v.tensor_tensor(g[5], g[0], g[2], ALU.min))
                own.link(v.tensor_tensor(g[6], g[1], g[3], ALU.max))
                own.link(v.tensor_tensor(g[5], g[5], g[6], ALU.max))
                own.link(v.tensor_tensor(g[4], g[4], g[5], ALU.add))

                def first_max(x, size, pre, wts, outp, mx):
                    x3 = x.rearrange("p (t e) -> p t e", t=TT)
                    o3 = outp.rearrange("p (t e) -> p t e", t=TT)
                    w3 = wts.rearrange("p (t e) -> p t e", t=TT)
                    own.link(v.tensor_reduce(mx, x3, AX, ALU.max))
                    own.link(v.tensor_tensor(w3, x3, mx.unsqueeze(2).to_broadcast([P, TT, size]), ALU.is_equal))
                    own.link(v.tensor_tensor(w3, w3, pre.unsqueeze(1).to_broadcast([P, TT, size]), ALU.mult))
                    own.link(v.tensor_reduce(mx, w3, AX, ALU.max))
                    own.link(v.tensor_tensor(o3, w3, mx.unsqueeze(2).to_broadcast([P, TT, size]), ALU.is_equal))

                countdown = K_[:, C_CD:C_CD + E]
                first_max(g[4], GROUPS, countdown[:, E - GROUPS:E], g[5], g[6], rs[:, 1, :])
                own.link(v.tensor_scalar(g[7], g[6], BIG, -BIG, ALU.mult, ALU.add))
                own.link(v.tensor_tensor(G4(3), s, g[6].unsqueeze(2).to_broadcast([P, TT * GROUPS, 4]), ALU.mult))
                own.link(v.tensor_tensor(G4(3), G4(3), g[7].unsqueeze(2).to_broadcast([P, TT * GROUPS, 4]), ALU.add))
                first_max(R[3], E, countdown, R[4], R[5], rs[:, 1, :])
                own.link(v.scalar_tensor_tensor(R[3], R[5], -BIG, R[3], ALU.mult, ALU.add))
                first_max(R[3], E, countdown, R[4], R[6], rs[:, 1, :])
                own.link(v.tensor_tensor(R[5], R[5], R[6], ALU.add))
                own.link(v.tensor_tensor(R[5], R[5], R[1], ALU.mult))
                own.link(v.tensor_reduce(rs[:, 1, :], V3(5), AX, ALU.add))
                own.link(v.reciprocal(rs[:, 2, :], rs[:, 1, :]))
                own.link(v.tensor_tensor(gates[:, :, :], V3(5), rs[:, 2, :].unsqueeze(2).to_broadcast([P, TT, E]), ALU.mult))

            def experts(i):
                route(i)
                first = at[("moe", i)]
                with dve.Fori(0, E // 2) as it:
                    for j in range(2):
                        for m in range(4):
                            dve.wait_ge(silu_h, it * 8 + (64 * i + 4 * j + m + 1))
                            v.tensor_tensor(hT[j][:, m, :], bank[m][:, SEQ:2 * SEQ], sil[m % 2], ALU.mult).then_inc(drained[m], 1)
                        for tt in range(TT):
                            for nh in range(2):
                                b = 4 + 2 * tt + nh
                                dve.wait_ge(filled[b], it * 2 + (first[b] + j + 1))
                                dve.wait_ge(drained[b], it * 2 + (first[b] + j))
                                sl = H[:, tt, nh * 512:(nh + 1) * 512]
                                v.scalar_tensor_tensor(sl, bank[b][:, :], gates[:, tt, bass.ds(it * 2 + j, 1)], sl,
                                                       ALU.mult, ALU.add).then_inc(drained[b], 1)
                for b in range(4, 8):
                    dve.wait_ge(drained[b], first[b] + E)

            ht_chunks(0)
            nn = 0
            nres = 1
            for i, kind in enumerate(kinds):
                j = kinds[:i].count(kind)
                if kind == 0:
                    delta(i, j)
                    X2 = view(8192, HEADS, P)
                    heads_norm(nn, lambda tt: O[:, :, tt * P:(tt + 1) * P],
                               lambda tt: gate[:, tt, :].rearrange("p (h d) -> p h d", h=HEADS), 1.0)
                    heads_out_T(i, nn, OT)
                    nn += 1
                elif kind == 1:
                    lam_init = 0.8 - 0.6 * math.exp(-0.3 * i)
                    attention(i, j, lam_init)
                    X2 = view(11264, HEADS, P)
                    heads_norm(nn, lambda tt: bO[:, :, tt * P:(tt + 1) * P],
                               lambda tt: bngb[:, :].unsqueeze(1).to_broadcast([P, HEADS, P]), 1.0 - lam_init)
                    heads_out_T(i, nn, bOT)
                    nn += 1
                else:
                    gmlp(i, j)
                dve.wait_ge(h_ready, 2 * nres)
                add_mixed(i)
                layer_norm()
                if 2 * i + 1 != last_phase:
                    ht_chunks(2 * i + 1)
                nres += 1
                if with_moe:
                    dve.wait_ge(h_ready, 2 * nres)
                    experts(i)
                    layer_norm()
                    nres += 1
                if i < n_layers - 1:
                    ht_chunks(2 * i + 2)

        @block.tensor
        def _(pe):
            mm, tr = nc.tensor.matmul, nc.tensor.transpose
            unit_n = 0

            def fill(*key):
                b, n = at[key]
                if n:
                    pe.wait_ge(drained[b], n)
                return bank[b]

            def done(ins, *key):
                ins.then_inc(filled[at[key][0]], 1)

            def next_unit():
                nonlocal unit_n
                s = unit_n % SLOTS
                pe.wait_ge(slot_in[s], 16 * (unit_n // SLOTS + 1))
                unit_n += 1
                return ring[s]

            def ht_chunks(phase):
                for k in range(KC):
                    ps = fill("ht", phase, k)
                    for tt in range(TT):
                        ins = tr(ps[:, tt * P:(tt + 1) * P], H[:, tt, k * P:(k + 1) * P], ident)
                    done(ins, "ht", phase, k)
                for k in range(KC):
                    wait_copy(pe, "ht", phase, k)

            def rows(dst, wt, n):
                for k in range(KC):
                    ins = mm(dst[:, 0:SEQ], wt[:, k, n * P:(n + 1) * P], HT[:, k, :], start=k == 0, stop=k == KC - 1)
                return ins

            def toks(dst, wt, tt):
                for k in range(KC):
                    ins = mm(dst[:, :], HT[:, k, tt * P:(tt + 1) * P], wt[:, k, :], start=k == 0, stop=k == KC - 1)
                return ins

            def heads_out(i, nn, X, XT):
                pe.wait_ge(o_ready, 2 * nn + 2)
                for g in range(4):
                    ps = fill("oT", i, g)
                    for h in (2 * g, 2 * g + 1):
                        for tt in range(TT):
                            c = (h % 2) * SEQ + tt * P
                            ins = tr(ps[:, c:c + P], X[:, h, tt * P:(tt + 1) * P], ident)
                    done(ins, "oT", i, g)
                for g in range(4):
                    wait_copy(pe, "oT", i, g)
                for nh in range(2):
                    wt = next_unit()
                    for tt in range(TT):
                        ps = fill("y", i, tt, nh)
                        for h in range(HEADS):
                            ins = mm(ps[:, :], XT[:, h, tt * P:(tt + 1) * P], wt[:, h, :], start=h == 0, stop=h == HEADS - 1)
                        done(ins, "y", i, tt, nh)

            def delta(i, j):
                ps = fill("ab", i)
                for tt in range(TT):
                    for k in range(KC):
                        ins = mm(ps[:, tt * 16:(tt + 1) * 16], HT[:, k, tt * P:(tt + 1) * P], wab[:, j, k, :], start=k == 0, stop=k == KC - 1)
                done(ins, "ab", i)
                for u in range(6):
                    wt = next_unit()
                    for c in range(4 * u, 4 * u + 4):
                        done(rows(fill("conv", i, c), wt, c % 4), "conv", i, c)
                        if c >= 16:
                            n = c - 16
                            ps = fill("ss", i, n)
                            pe.wait_ge(squares, 8 * j + n + 1)
                            done(mm(ps[:, :], ones[:, :], sq[n % 2], start=True, stop=True), "ss", i, n)
                ps = fill("G", i)
                pe.wait_ge(ab_mid, 2 * j + 2)
                ins = mm(ps[:, 0:16], cum, abr[:, 7, :, :], start=True, stop=True)
                ins = mm(ps[:, 16:32], blk, abr[:, 7, :, :], start=True, stop=True)
                done(ins, "G", i)
                for nh in range(2):
                    wt = next_unit()
                    for tt in range(TT):
                        done(toks(fill("gate", i, tt, nh), wt, tt), "gate", i, tt, nh)
                pe.wait_ge(qk_normed, 8 * j + 8)
                for tt in range(TT):
                    ts = slice(tt * P, (tt + 1) * P)
                    for hg in range(2):
                        ps = fill("GB", i, tt, hg)
                        for h in range(4 * hg, 4 * hg + 4):
                            ins = mm(ps[:, (h % 4) * P:(h % 4 + 1) * P], abr[:, 7, tt, h:h + 1].to_broadcast([P, P]), cum, start=True, stop=True)
                        done(ins, "GB", i, tt, hg)
                    for hg in range(2):
                        for key, right in (("kk", kT), ("qk", qT)):
                            ps = fill(key, i, tt, hg)
                            for h in range(4 * hg, 4 * hg + 4):
                                ins = mm(ps[:, (h % 4) * P:(h % 4 + 1) * P], kT[:, h, ts], right[:, h, ts], start=True, stop=True)
                            done(ins, key, i, tt, hg)
                    pe.wait_ge(silu_qkv, 18 * j + 18)
                    for hg in range(2):
                        for key, src in (("Ktok", kT), ("Vtok", vT)):
                            ps = fill(key, i, tt, hg)
                            for h in range(4 * hg, 4 * hg + 4):
                                ins = tr(ps[:, (h % 4) * P:(h % 4 + 1) * P], src[:, h, ts], ident)
                            done(ins, key, i, tt, hg)
                    for hg in range(2):
                        ps = fill("T0", i, tt, hg)
                        pe.wait_ge(inv_done, 4 * j + 2 * tt + hg + 1)
                        for h in range(4 * hg, 4 * hg + 4):
                            ins = tr(ps[:, (h % 4) * P:(h % 4 + 1) * P], Ti[:, h, :], ident)
                        done(ins, "T0", i, tt, hg)
                    for lv in range(1, LEVELS):
                        for hg in range(2):
                            ps = fill("Y", i, tt, lv, hg)
                            pe.wait_ge(masked, 20 * j + 10 * tt + 2 * (lv - 1) + hg + 1)
                            wait_copy(pe, "T0", i, tt, hg) if lv == 1 else wait_copy(pe, "T", i, tt, lv - 1, hg)
                            for h in range(4 * hg, 4 * hg + 4):
                                ins = mm(ps[:, (h % 4) * P:(h % 4 + 1) * P], AM[:, h, :], T[:, h, :], start=True, stop=True)
                            done(ins, "Y", i, tt, lv, hg)
                        for hg in range(2):
                            wait_copy(pe, "Y", i, tt, lv, hg)
                            if lv > 1:
                                wait_copy(pe, "TT", i, tt, lv - 1, hg)
                            ps = fill("TT", i, tt, lv, hg)
                            for h in range(4 * hg, 4 * hg + 4):
                                ins = mm(ps[:, (h % 4) * P:(h % 4 + 1) * P], Y[:, h, :], Ti[:, h, :], start=True, stop=True)
                            done(ins, "TT", i, tt, lv, hg)
                            if lv < LEVELS - 1:
                                ps = fill("T", i, tt, lv, hg)
                                for h in range(4 * hg, 4 * hg + 4):
                                    ins = mm(ps[:, (h % 4) * P:(h % 4 + 1) * P], Ti[:, h, :], Y[:, h, :], start=True, stop=True)
                                done(ins, "T", i, tt, lv, hg)
                    for hg in range(2):
                        ps = fill("W", i, tt, hg)
                        pe.wait_ge(kscaled, 4 * j + 2 * tt + hg + 1)
                        wait_copy(pe, "TT", i, tt, LEVELS - 1, hg)
                        for h in range(4 * hg, 4 * hg + 4):
                            ins = mm(ps[:, (h % 4) * P:(h % 4 + 1) * P], kG[:, h, :], Ti[:, h, :], start=True, stop=True)
                        done(ins, "W", i, tt, hg)
                    wait_copy(pe, "Vtok", i, tt, 0)
                    wait_copy(pe, "Vtok", i, tt, 1)
                    for hg in range(2):
                        fill("o", i, tt, hg)
                    pe.wait_ge(qdec, 4 * j + 2 * tt + 2)
                    for c in range(2):
                        rr = slice(64 * c, 64 * c + 64)
                        last = (tt, c) == (TT - 1, 1)
                        for hg in range(2):
                            ps = fill("vn", i, tt, c, hg)
                            po = bank[at[("o", i, tt, hg)][0]]
                            if c == 0:
                                for h in range(4 * hg, 4 * hg + 4):
                                    ins = mm(ps[:, (h % 4) * P:(h % 4 + 1) * P], Ti[:, h, :], Vtok[:, h, :], start=h % 4 == 0, stop=False, skip_group_check=True)
                                wait_copy(pe, "W", i, tt, hg)
                            if (tt, c) != (0, 0):
                                wait_copy(pe, "su", i, *((tt, 0) if c else (tt - 1, 1)), hg)
                            for h in range(4 * hg, 4 * hg + 4):
                                mm(po[rr, (h % 4) * P:(h % 4 + 1) * P], qT[:, h, tt * P + 64 * c:tt * P + 64 * c + 64], S[:, h, :],
                                   start=h % 4 == 0, stop=False, skip_group_check=True)
                            for h in range(4 * hg, 4 * hg + 4):
                                ins = mm(ps[rr, (h % 4) * P:(h % 4 + 1) * P], NWT[:, h, rr], S[:, h, :], start=False, stop=True, skip_group_check=True)
                            done(ins, "vn", i, tt, c, hg)
                        for hg in range(2):
                            wait_copy(pe, "vn", i, tt, c, hg)
                            if last:
                                continue
                            ps = fill("su", i, tt, c, hg)
                            for h in range(4 * hg, 4 * hg + 4):
                                ins = mm(ps[:, (h % 4) * P:(h % 4 + 1) * P], kd[rr, h, :], vnew[rr, h, :], start=True, stop=True)
                            done(ins, "su", i, tt, c, hg)
                    for hg in range(2):
                        po = bank[at[("o", i, tt, hg)][0]]
                        wait_copy(pe, "qk", i, tt, hg)
                        for h in range(4 * hg, 4 * hg + 4):
                            ins = mm(po[:, (h % 4) * P:(h % 4 + 1) * P], attnT[:, h, :], vnew[:, h, :], start=False, stop=True, skip_group_check=True)
                        done(ins, "o", i, tt, hg)

            def attention(i, j):
                for u in range(4):
                    wt = next_unit()
                    for c in range(4 * u, 4 * u + 4):
                        done(rows(fill("qkT", i, c), wt, c % 4), "qkT", i, c)
                        if 4 <= c < 10:
                            n = c - 4
                            if n == 0:
                                pe.wait_ge(toep_in, 48)
                            done(mm(fill("flip", i, n)[:, :], flip, TBr[:, n * 512:(n + 1) * 512], start=True, stop=True), "flip", i, n)
                for nh in range(2):
                    wt = next_unit()
                    for tt in range(TT):
                        done(toks(fill("v", i, tt, nh), wt, tt), "v", i, tt, nh)
                for c in range(16):
                    wait_copy(pe, "qkT", i, c)
                for nh in range(2):
                    for tt in range(TT):
                        wait_copy(pe, "v", i, tt, nh)
                for h in range(HEADS + 2):
                    if h < HEADS:
                        for m in range(2):
                            ps = fill("lg", i, h, m)
                            ms = slice(64 * m, 64 * m + 64)
                            mm(ps[:, 0:P], qT[ms, h, 0:P], kT[ms, h, 0:P], start=True, stop=True)
                            done(mm(ps[:, P:TOEP], qT[ms, h, P:SEQ], kT[ms, h, :], start=True, stop=True), "lg", i, h, m)
                    if 1 <= h <= HEADS:
                        g = h - 1
                        ps = fill("pT", i, g)
                        pe.wait_ge(pa_ready, HEADS * j + g + 1)
                        for b in range(3):
                            ins = tr(ps[:, b * P:(b + 1) * P], PA[g % 2][:, b * P:(b + 1) * P], ident)
                        done(ins, "pT", i, g)
                    if h >= 2:
                        g = h - 2
                        ps = fill("ob", i, g)
                        wait_copy(pe, "pT", i, g)
                        gs = slice(g * P, (g + 1) * P)
                        mm(ps[:, 0:P], PT[g % 2][:, 0:P], Vb[:, 0, gs], start=True, stop=True)
                        mm(ps[:, P:SEQ], PT[g % 2][:, P:2 * P], Vb[:, 0, gs], start=True, stop=False)
                        done(mm(ps[:, P:SEQ], PT[g % 2][:, 2 * P:TOEP], Vb[:, 1, gs], start=False, stop=True), "ob", i, g)

            def gmlp(i, j):
                pe.wait_ge(cpar_in, 48)
                for g in range(2):
                    ps = fill("wsT", i, g)
                    for n in range(4):
                        ins = tr(ps[:, n * P:(n + 1) * P], ws[:, 4 * g + n, :], ident)
                    done(ins, "wsT", i, g)
                for u in (4, 5, 6, 7, 0, 1, 2, 3):
                    wt = next_unit()
                    for tt in range(TT):
                        done(toks(fill("z", i, u, tt), wt, tt), "z", i, u, tt)
                for g in range(2):
                    wait_copy(pe, "wsT", i, g)
                for tt in range(TT):
                    pe.wait_ge(v_ln, 2 * j + tt + 1)
                    for g2 in range(4):
                        ps = fill("mix", i, tt, g2)
                        for g in (2 * g2, 2 * g2 + 1):
                            ins = mm(ps[:, (g % 2) * 256:(g % 2 + 1) * 256], wsT[:, g, :], v_[:, tt, g * 256:(g + 1) * 256], start=True, stop=True)
                        done(ins, "mix", i, tt, g2)
                for tt in range(TT):
                    for g2 in range(4):
                        wait_copy(pe, "mix", i, tt, g2)
                for g in range(8):
                    ps = fill("uT", i, g)
                    for n in range(2):
                        for tt in range(TT):
                            c = n * SEQ + tt * P
                            ins = tr(ps[:, c:c + P], u_[:, tt, (2 * g + n) * P:(2 * g + n + 1) * P], ident)
                    done(ins, "uT", i, g)
                for g in range(8):
                    wait_copy(pe, "uT", i, g)
                for nh in range(2):
                    pss = [fill("y", i, tt, nh) for tt in range(TT)]
                    wts = [next_unit(), next_unit()]
                    for tt in range(TT):
                        for k in range(16):
                            ins = mm(pss[tt][:, :], uT[:, k, tt * P:(tt + 1) * P], wts[k // 8][:, k % 8, :], start=k == 0, stop=k == 15)
                        done(ins, "y", i, tt, nh)

            def experts(i):
                nonlocal unit_n
                ps = fill("rt", i)
                for tt in range(TT):
                    for k in range(KC):
                        ins = mm(ps[:, tt * E:(tt + 1) * E], HT[:, k, tt * P:(tt + 1) * P], wr[:, k, :], start=k == 0, stop=k == KC - 1)
                done(ins, "rt", i)
                first = at[("moe", i)]
                with pe.Fori(0, E // 2) as it:
                    for j in range(2):
                        s1, s3, s2 = [(unit_n + 3 * j + n) % SLOTS for n in range(3)]
                        c1, c3, c2 = [(unit_n + 3 * j + n) // SLOTS for n in range(3)]
                        pe.wait_ge(slot_in[s1], it * 16 + 16 * (c1 + 1))
                        pe.wait_ge(slot_in[s3], it * 16 + 16 * (c3 + 1))
                        for m in range(4):
                            pe.wait_ge(drained[m], it * 2 + (first[m] + j))
                            for half, s in ((0, s1), (1, s3)):
                                for k in range(KC):
                                    ins = mm(bank[m][:, half * SEQ:(half + 1) * SEQ], ring[s][:, k, m * P:(m + 1) * P], HT[:, k, :],
                                             start=k == 0, stop=k == KC - 1)
                            ins.then_inc(filled[m], 1)
                        pe.wait_ge(slot_in[s2], it * 16 + 16 * (c2 + 1))
                        w2 = ring[s2][:, :, :].rearrange("p a b -> p (a b)").rearrange("p (m n) -> p m n", m=4)
                        for m in range(4):
                            pe.wait_ge(drained[m], it * 2 + (first[m] + j + 1))
                        for tt in range(TT):
                            for nh in range(2):
                                b = 4 + 2 * tt + nh
                                pe.wait_ge(drained[b], it * 2 + (first[b] + j))
                                for m in range(4):
                                    ins = mm(bank[b][:, :], hT[j][:, m, tt * P:(tt + 1) * P], w2[:, m, nh * 512:(nh + 1) * 512], start=m == 0, stop=m == 3)
                                ins.then_inc(filled[b], 1)
                unit_n += 3 * E

            pe.wait_ge(params_in, N_PARAMS)
            pe.wait_ge(consts_set, 4)
            ps = fill("cols")
            tr(ps[:, 0:P], lnrows[:, :], ident)
            for j in range(2):
                tr(ps[:, P * (j + 1):P * (j + 1) + 96], convrows[:, j, :], ident[0:96, 0:96])
            done(tr(ps[:, 384:392], bsrow[:, :], ident[0:HEADS, 0:HEADS]), "cols")
            done(mm(fill("relrow")[0:HEADS, 0:TOEP], rel33[:, :], onehot, start=True, stop=True), "relrow")
            pe.wait_ge(x_ready, 16)
            ht_chunks(0)
            nn = 0
            lnn = 0
            for i, kind in enumerate(kinds):
                j = kinds[:i].count(kind)
                if kind == 0:
                    delta(i, j)
                    heads_out(i, nn, O, OT)
                    nn += 1
                elif kind == 1:
                    attention(i, j)
                    heads_out(i, nn, bO, bOT)
                    nn += 1
                else:
                    gmlp(i, j)
                lnn += 1
                if 2 * i + 1 != last_phase:
                    pe.wait_ge(xhat_ready, 2 * lnn)
                    ht_chunks(2 * i + 1)
                if with_moe:
                    experts(i)
                    lnn += 1
                if i < n_layers - 1:
                    if with_moe:
                        pe.wait_ge(xhat_ready, 2 * lnn)
                    ht_chunks(2 * i + 2)


N_PARAMS = 16 * 22


def constants():
    import numpy as np

    c = np.zeros((P, C_ALL), np.float32)
    m, t = np.arange(P)[:, None], np.arange(P)[None, :]
    same = m // CHUNK == t // CHUNK
    c[:, C_ID:C_ID + P] = m == t
    c[:, C_NEG:C_NEG + P] = np.where(same & (t >= m), 0.0, -BIG)
    for lv in range(LEVELS):
        b = 1 << lv
        c[:, C_LV + lv * P:C_LV + (lv + 1) * P] = (m // (2 * b) == t // (2 * b)) & (m // b % 2 == 0) & (t // b % 2 == 1)
    c[:, C_CUM:C_CUM + P] = same & (m <= t)
    c[:, C_BLK:C_BLK + P] = same
    c[:, C_TRI:C_TRI + P] = m <= t
    exact = REL_BUCKETS // 2
    n = 255 - np.arange(TOEP)
    large = exact + (np.log(np.maximum(n, 1).astype(np.float32) / np.float32(exact)) / np.float32(math.log(128 / exact))
                     * np.float32(REL_BUCKETS - exact)).astype(np.int32)
    bucket = np.where(n < 0, REL_BUCKETS, np.where(n < exact, np.maximum(n, 0), np.minimum(large, REL_BUCKETS - 1)))
    c[bucket, C_OH + np.arange(TOEP)] = 1.0
    c[:, C_FLIP:C_FLIP + P] = m + t == P - 1
    c[:, C_CD:C_CD + E] = E - np.arange(E)
    return c


_INS = ["x", "ln_mix_g", "ln_mix_b", "ln_ffn_g", "ln_ffn_b", "a_w_in", "a_conv", "a_a_log", "a_dt_bias", "a_norm_g",
        "a_w_out", "b_w_in", "b_lambda", "b_norm_g", "b_w_out", "rel_bias", "c_w_in", "c_ln_g", "c_ln_b", "c_w_s",
        "c_b_s", "c_w_out", "w_router", "router_bias", "e_w1", "e_w3", "e_w2"]


def kernel(**inputs):
    import numpy as np
    import concourse.bacc as bacc
    from concourse.bass_utils import run_bass_kernel_spmd

    nc = bacc.Bacc("TRN2", target_bir_lowering=False, num_devices=1)
    arrays = {f"in_{name}": np.ascontiguousarray(inputs[name]) for name in _INS}
    arrays["in_consts"] = constants()
    w = {name[3:]: nc.dram_tensor(name, a.shape, mybir.dt.from_np(a.dtype), kind="ExternalInput").ap()
         for name, a in arrays.items()}
    out = nc.dram_tensor("out", [1, SEQ, D], F32, kind="ExternalOutput").ap()
    trunk(nc, w, out)
    r = run_bass_kernel_spmd(nc, [arrays], core_ids=[0])
    return r.results[0]["out"]
```

```python
import math
from contextlib import ExitStack

import concourse.bass as bass
from concourse import mybir

F32 = mybir.dt.float32
ACT = mybir.ActivationFunctionType
ALU = mybir.AluOpType
AX = mybir.AxisListType.X

P = 128
D = 1024
SEQ = 256
TT = SEQ // P
KC = D // P
DEPTH = 4
HEADS = 8
CHUNK = 64
E = 16
GROUPS = 4
DE = 512
SLOTS = 6
UNIT = 4096
ALPHA = float((2 * DEPTH) ** 0.25)
EPS = 1e-5
L2EPS = 1e-6
BIG = 1e30
LEVELS = 6
CAP = 64
PASSES = SEQ // CAP
H_STEPS = 7
Y_STEPS = 6
PAIR_TURNS = (1, 1, 4, 2, 1, 1, 1, 1)
REL_BUCKETS = 32
TOEP = 384

C_ID, C_NEG, C_LV, C_CUM, C_BLK, C_TRI, C_CD = 0, 128, 256, 1024, 1152, 1280, 1408
C_IOTA = C_CD + E
C_SB = C_IOTA + 2 * CAP
C_OH = C_SB
C_FLIP = C_OH + TOEP
C_ALL = C_FLIP + P

ALL_KINDS = tuple(i % 3 for i in range(DEPTH))


class Turns:

    def __init__(self):
        self.count = [0] * 8
        self.at = {}

    def take(self, bank, *key):
        self.at[key] = (bank, self.count[bank])
        self.count[bank] += 1

    def loop(self, key, per_pass, passes):
        self.at[key] = list(self.count)
        self.count = [c + n * passes for c, n in zip(self.count, per_pass)]


def plan(kinds, with_moe, w):
    turns, units = Turns(), []

    def unit(src, last):
        units.append((src, last))

    def heads_out(i, w_out):
        for g in range(4):
            turns.take(g, "oT", i, g)
        for nh in range(2):
            for tt in range(TT):
                turns.take(4 + 2 * tt + nh, "y", i, tt, nh)
            unit(w_out[:, nh * 512:(nh + 1) * 512].rearrange("(k p) n -> p k n", p=P), ("y", i, TT - 1, nh))

    for k in range(KC):
        turns.take(k, "ht", 0, k)
    turns.take(0, "cols")
    turns.take(1, "relrow")
    for i, kind in enumerate(kinds):
        j = kinds[:i].count(kind)
        if kind == 0:
            win = w["a_w_in"][j]
            turns.take(0, "ab", i)
            for u in range(6):
                for c in range(4 * u, 4 * u + 4):
                    turns.take(2 + c % 4, "conv", i, c)
                    if c >= 16:
                        turns.take(6 + c % 2, "ss", i, c - 16)
                unit(win[:, u * 512:(u + 1) * 512].rearrange("(k p) n -> p k n", p=P), ("conv", i, 4 * u + 3))
            turns.take(1, "G", i)
            for nh in range(2):
                for tt in range(TT):
                    turns.take(tt, "gate", i, tt, nh)
                u = 6 + nh
                unit(win[:, u * 512:(u + 1) * 512].rearrange("(k p) n -> p k n", p=P), ("gate", i, TT - 1, nh))
            for tt in range(TT):
                for hg in range(2):
                    turns.take(hg, "GB", i, tt, hg)
                for hg in range(2):
                    turns.take(2 + hg, "kk", i, tt, hg)
                    turns.take(4 + hg, "qk", i, tt, hg)
                for hg in range(2):
                    turns.take(6, "Ktok", i, tt, hg)
                    turns.take(7, "Vtok", i, tt, hg)
                for hg in range(2):
                    turns.take(hg, "T0", i, tt, hg)
                for lv in range(1, LEVELS):
                    for hg in range(2):
                        turns.take(hg, "Y", i, tt, lv, hg)
                    for hg in range(2):
                        turns.take(2 + hg, "TT", i, tt, lv, hg)
                        if lv < LEVELS - 1:
                            turns.take(4 + hg, "T", i, tt, lv, hg)
                for hg in range(2):
                    turns.take(6 + hg, "W", i, tt, hg)
                for c in range(2):
                    for hg in range(2):
                        turns.take(hg, "vn", i, tt, c, hg)
                    for hg in range(2):
                        if (tt, c) != (TT - 1, 1):
                            turns.take(4 + hg, "su", i, tt, c, hg)
                for hg in range(2):
                    turns.take(2 + hg, "o", i, tt, hg)
            heads_out(i, w["a_w_out"][j])
        elif kind == 1:
            win = w["b_w_in"][j]
            for u in range(4):
                for c in range(4 * u, 4 * u + 4):
                    turns.take(c % 4, "qkT", i, c)
                    if 4 <= c < 10:
                        turns.take(4 + c % 4, "flip", i, c - 4)
                unit(win[:, u * 512:(u + 1) * 512].rearrange("(k p) n -> p k n", p=P), ("qkT", i, 4 * u + 3))
            for nh in range(2):
                for tt in range(TT):
                    turns.take(4 + 2 * nh + tt, "v", i, tt, nh)
                u = 4 + nh
                unit(win[:, u * 512:(u + 1) * 512].rearrange("(k p) n -> p k n", p=P), ("v", i, TT - 1, nh))
            for h in range(-2, HEADS + 1):
                if 0 <= h < HEADS:
                    turns.take(4 + h % 2, "pT", i, h)
                if h + 2 < HEADS:
                    for m in range(2):
                        turns.take(2 * (h % 2) + m, "lg", i, h + 2, m)
                if h >= 1:
                    turns.take(6 + (h - 1) % 2, "ob", i, h - 1)
            heads_out(i, w["b_w_out"][j])
        else:
            win, wout = w["c_w_in"][j], w["c_w_out"][j]
            for u in (4, 5, 6, 7, 0, 1, 2, 3):
                for tt in range(TT):
                    turns.take(2 + (2 * u + tt) % 4, "z", i, u, tt)
                if u == 7:
                    for g in range(2):
                        turns.take(g, "wsT", i, g)
                unit(win[:, u * 512:(u + 1) * 512].rearrange("(k p) n -> p k n", p=P), ("z", i, u, TT - 1))
            for tt in range(TT):
                for g in range(4):
                    turns.take(g, "mix", i, tt, g)
            for g in range(8):
                turns.take(g % 4, "uT", i, g)
            for nh in range(2):
                for tt in range(TT):
                    turns.take(4 + 2 * tt + nh, "y", i, tt, nh)
                for kh in range(2):
                    unit(wout[kh * 1024:(kh + 1) * 1024, nh * 512:(nh + 1) * 512].rearrange("(k p) n -> p k n", p=P),
                         ("y", i, TT - 1, nh))
        for k in range(KC):
            turns.take(k, "ht", 2 * i + 1, k)
        if with_moe:
            turns.take(0, "rt", i)
            turns.take(1, "rank", i)
            for n in range(2):
                turns.take(n, "first", i, n)
            turns.loop(("moe", i), PAIR_TURNS, E // 2)
            units.append(("moe", i))
        if i < len(kinds) - 1:
            for k in range(KC):
                turns.take(k, "ht", 2 * i + 2, k)
    return turns.at, units


def trunk(nc, w, out, kinds=ALL_KINDS, with_moe=True):
    at, units = plan(kinds, with_moe, w)
    n_layers = len(kinds)
    with ExitStack() as ctx:
        def sb(name, shape):
            return ctx.enter_context(nc.sbuf_tensor(name, shape, F32))

        def sem(name):
            return ctx.enter_context(nc.semaphore(name))

        ring = [sb(f"ring{s}", [P, 8, 512]) for s in range(SLOTS)]
        H = sb("H", [P, TT, D])
        HT = sb("HT", [P, KC, SEQ])
        gB = sb("gB", [P, D])
        bB = sb("bB", [P, D])
        K_ = sb("consts_sb", [P, C_SB])
        ident = K_[:, C_ID:C_ID + P]
        neg_mask = K_[:, C_NEG:C_NEG + P]
        cum = K_[:, C_CUM:C_CUM + P]
        blk = K_[:, C_BLK:C_BLK + P]
        tri = K_[:, C_TRI:C_TRI + P]
        onehot = bB[0:REL_BUCKETS + 1, 0:TOEP]
        work = sb("work", [P, 18432])
        lnrows = gB[:, 0:P]
        lncols = sb("lncols", [P, P])
        convrows = gB[0:96, P:3 * P].rearrange("p (a b) -> p a b", a=2)
        bsrow = gB[0:HEADS, 3 * P:4 * P]
        relrow = gB[0:HEADS, 4 * P:4 * P + TOEP]
        convcols = sb("convcols", [P, 2, 96])
        ones = sb("ones", [P, P])
        wab = sb("wab", [P, 2, KC, 16])
        alog = sb("alog", [P, 2, HEADS])
        dtb = sb("dtb", [P, 2, HEADS])
        angb = sb("angb", [P, 2, P])
        lamb = sb("lamb", [P, 4, 64])
        bngb = sb("bngb", [P, P])
        rel33 = sb("rel33", [REL_BUCKETS + 1, HEADS])
        bscol = sb("bscol", [P, HEADS])
        wr = sb("wr", [P, KC, E])
        rbias = sb("rbias", [P, E])
        epsc = sb("epsc", [P, 2])
        warm = sb("warm", [P, 1])
        stats = sb("stats", [P, TT, 24])
        mv = sb("mv", [P, TT, 2])
        rs = sb("rs", [P, 4, TT])
        gates = sb("gates", [P, TT, E])
        place = sb("place", [P, TT, PASSES * (E + 2)])
        counts = ctx.enter_context(nc.sbuf_tensor("counts", [1, E], mybir.dt.int32))
        abr = sb("abr", [P, 8, TT, HEADS])
        gsc = sb("gsc", [P, 8, TT, HEADS])
        egl = sb("egl", [P, HEADS, 2])
        ssq = sb("ssq", [P, 4, TT, HEADS])
        lm = sb("lm", [P, 8])
        sm = sb("sm", [P, HEADS, 8])

        def view(lo, a, b):
            return work[:, lo:lo + a * b].rearrange("p (a b) -> p a b", a=a)

        qT, kT, vT = view(0, HEADS, SEQ), view(2048, HEADS, SEQ), view(4096, HEADS, SEQ)
        gate = view(6144, TT, D)
        Ktok, Vtok = view(8192, HEADS, P), view(9216, HEADS, P)
        AT, attnT = view(10240, HEADS, P), view(11264, HEADS, P)
        T, Ti = view(12288, HEADS, P), view(13312, HEADS, P)
        Y, S = view(14336, HEADS, P), view(15360, HEADS, P)
        AM, DT = view(16384, HEADS, P), view(17408, HEADS, P)
        NWT, kd, kG, vnew, EGB = T, Y, AM, DT, Y
        cv = [work[:, 12288 + 256 * n:12544 + 256 * n] for n in range(4)]
        sq = [work[:, 13312 + 512 * n:13824 + 512 * n] for n in range(2)]
        lnr = [work[:, 14336 + 512 * n:14848 + 512 * n] for n in range(2)]
        O = vT
        OT = kT
        TB = work[:, 8192:8192 + HEADS * TOEP].rearrange("p (h k) -> p h k", h=HEADS)
        TBr = work[:, 15360:18432]
        flip = work[:, 11264:11392]
        L = [work[:, 11264 + 768 * n:11264 + 768 * n + 768].rearrange("p (m k) -> p m k", m=2) for n in range(2)]
        PA = [work[:, 12800 + 384 * n:12800 + 384 * n + 384] for n in range(2)]
        PT = [work[:, 13568 + 384 * n:13568 + 384 * n + 384] for n in range(2)]
        bO = view(14336, HEADS, SEQ)
        Vb = view(6144, TT, D)
        bOT = view(4096, HEADS, SEQ)
        u_ = view(0, TT, 2048)
        v_ = view(4096, TT, 2048)
        gC, bC = work[:, 8192:10240], work[:, 10240:12288]
        ws = view(12288, HEADS, P)
        wsT = view(13312, HEADS, P)
        uT = view(4096, 16, SEQ)
        iota2 = K_[:, C_IOTA:C_IOTA + 2 * CAP]
        XH = view(0, TT, D)
        rt = view(8192, 8, TT * E)
        rg = view(8448, 8, TT * GROUPS)

        sel, selg, selgT = view(2048, TT, 2 * CAP), view(2304, TT, 2 * CAP), work[:, 2560:2816]
        x_ = view(2816, KC, 2 * CAP)
        sil, h_, hT = work[:, 3840:4352], work[:, 4352:4864], view(4864, 4, CAP)
        y_ = work[:, 5120:6144]
        m_sel, m_x = view(6144, TT, CAP), view(6272, KC, CAP)
        m_sil, m_turned, m_y = [work[:, 8704 + 512 * n:9216 + 512 * n] for n in range(3)]
        m_selg = [None] + [view(10240 + 256 * n, TT, 2 * CAP) for n in range(PASSES - 1)]
        m_h = [None] + [work[:, 11008 + 512 * n:11520 + 512 * n] for n in range(PASSES - 1)]

        bank = [ctx.enter_context(nc.psum_tensor(f"bank{b}", [P, 512], F32)) for b in range(8)]
        filled = [sem(f"filled{b}") for b in range(8)]
        drained = [sem(f"drained{b}") for b in range(8)]
        slot_in = [sem(f"slot_in{s}") for s in range(SLOTS)]
        params_in = sem("params_in")
        masks_in = sem("masks_in")
        x_ready = sem("x_ready")
        rows_in = sem("rows_in")
        rel_out = sem("rel_out")
        toep_in = sem("toep_in")
        cpar_in = sem("cpar_in")
        consts_set = sem("consts_set")
        var_ready = sem("var_ready")
        rstd_ready = sem("rstd_ready")
        xhat_ready = sem("xhat_ready")
        h_ready = sem("h_ready")
        mask_ready = sem("mask_ready")
        sel_ready = sem("sel_ready")
        silu_h = sem("silu_h")
        x_scaled = sem("x_scaled")
        baton = sem("baton")
        tap_ready = sem("tap_ready")
        silu_qkv = sem("silu_qkv")
        squares = sem("squares")
        rnorm = sem("rnorm")
        qk_normed = sem("qk_normed")
        ab_exp = sem("ab_exp")
        ab_mid = sem("ab_mid")
        gcol_ready = sem("gcol_ready")
        gexp = sem("gexp")
        gate_silu = sem("gate_silu")
        gate_ready = sem("gate_ready")
        egb_ready = sem("egb_ready")
        decay = sem("decay")
        qdec = sem("qdec")
        masked = sem("masked")
        inv_done = sem("inv_done")
        kscaled = sem("kscaled")
        kd_ready = sem("kd_ready")
        s_scaled = sem("s_scaled")
        ss_ready = sem("ss_ready")
        rms_ready = sem("rms_ready")
        o_ready = sem("o_ready")
        lam_dot = sem("lam_dot")
        lam_exp = sem("lam_exp")
        nmax = sem("nmax")
        probs = sem("probs")
        pa_ready = sem("pa_ready")
        v_ln = sem("v_ln")
        out_done = sem("out_done")
        v_chain = sem("v_chain")
        a_chain = sem("a_chain")
        p_chain = sem("p_chain")

        class Chain:

            def __init__(self, eng, s):
                self.eng, self.s, self.n = eng, s, 0

            def then(self, ins):
                ins.then_inc(self.s, 1)
                self.n += 1

            def wait(self):
                self.eng.wait_ge(self.s, self.n)

            def link(self, ins):
                self.then(ins)
                self.wait()

        def wait_data(eng, *key):
            b, n = at[key]
            eng.wait_ge(filled[b], n + 1)
            return bank[b]

        def wait_copy(eng, *key):
            b, n = at[key]
            eng.wait_ge(drained[b], n + 1)

        def emptied(ins, *key):
            ins.then_inc(drained[at[key][0]], 1)

        scratch = nc.dram_tensor("toeplitz_rows", [HEADS, TOEP], F32, kind="Internal").ap()
        lnp = {1: ("ln_mix_g", "ln_mix_b"), 0: ("ln_ffn_g", "ln_ffn_b")}
        block = ctx.enter_context(nc.Block())

        @block.sync
        def _(sp):
            def load(s, src):
                sp.dma_start(ring[s][:, :, :] if len(src.shape) == 3 and src.shape[1] == 8
                             else ring[s][:, :, :].rearrange("p a b -> p (a b)").rearrange("p (m n) -> p m n", m=4), src).then_inc(slot_in[s], 16)

            def expert_src(i, e, part):
                if part == 2:
                    return w["e_w2"][i, e].rearrange("(m p) n -> p m n", p=P)
                return w["e_w1" if part == 0 else "e_w3"][i, e].rearrange("(k p) n -> p k n", p=P)

            def release(last):
                if last[0] == "moe":
                    _, i, j, part = last
                    first = at[("moe", i)]
                    if part == 2:
                        sp.wait_ge(filled[3], first[3] + E - 2 + j + 1)
                    else:
                        sp.wait_ge(filled[2], first[2] + 2 * E - 4 + 2 * j + 2)
                else:
                    b, n = at[last]
                    sp.wait_ge(filled[b], n + 1)

            n = 0
            held = []
            for src, last in units:
                if n == 1:
                    sp.wait_ge(params_in, N_PARAMS)
                if isinstance(src, str):
                    i = last
                    for j in range(2):
                        for part in range(3):
                            if n >= SLOTS:
                                release(held[n - SLOTS])
                            load(n % SLOTS, expert_src(i, j, part))
                            held.append(("moe", i, j, part))
                            n += 1
                    first = at[("moe", i)]
                    with sp.Fori(1, E // 2) as it:
                        for j in range(2):
                            for part in range(3):
                                if part == 2:
                                    sp.wait_ge(filled[3], it * 2 + (first[3] - 2 + j + 1))
                                else:
                                    sp.wait_ge(filled[2], it * 4 + (first[2] - 4 + 2 * j + 2))
                                load((n + 3 * j + part) % SLOTS, expert_src(i, it * 2 + j, part))
                    held += [("moe", i, j, part) for _ in range(E // 2 - 1) for j in range(2) for part in range(3)]
                    n += 6 * (E // 2 - 1)
                    continue
                if n >= SLOTS:
                    release(held[n - SLOTS])
                load(n % SLOTS, src)
                held.append(last)
                n += 1
            for tt in range(TT):
                sp.wait_ge(h_ready, 2 * (2 * n_layers - (0 if with_moe else n_layers)) + tt + 1)
                sp.dma_start(out[0, tt * P:(tt + 1) * P, :], H[:, tt, :]).then_inc(out_done, 16)
            sp.wait_ge(out_done, 16 * TT)

        phases = []
        for i in range(n_layers):
            phases.append((2 * i + 1, 1, i))
            if with_moe:
                phases.append((2 * i + 2, 0, i))
        last_phase = phases[-1][0]

        def bcast(src, n):
            return bass.AP(tensor=src.tensor, offset=src.offset, ap=[[0, P], [1, n]])

        @block.gpsimd
        def _(pool):
            own = Chain(pool, p_chain)
            pool.memset(rel33[:, :], -BIG).then_inc(consts_set, 1)
            pool.memset(ones[:, :], 1.0).then_inc(consts_set, 1)
            pool.memset(epsc[:, 0:1], EPS).then_inc(consts_set, 1)
            pool.memset(epsc[:, 1:2], L2EPS).then_inc(consts_set, 1)
            pool.wait_ge(x_ready, 16)
            for k in range(KC):
                wait_data(pool, "ht", 0, k)
            for tt in range(TT):
                pool.tensor_scalar(H[:, tt, :], H[:, tt, :], ALPHA, None, ALU.mult).then_inc(h_ready, 1)

            ph = 0

            def residual(phase, which, i):
                nonlocal ph
                g, b = lnp[which]
                if ph:
                    own.wait()
                else:
                    wait_data(pool, "cols")
                    pool.wait_ge(rel_out, 16)
                pool.dma_start(gB[:, :], bcast(w[g][i], D)).then_inc(rows_in, 16)
                pool.dma_start(bB[:, :], bcast(w[b][i], D)).then_inc(rows_in, 16)
                ph += 1
                pool.wait_ge(rows_in, 32 * ph)
                if phase == last_phase:
                    return
                src = XH if which else H
                if src is H:
                    for k in range(KC):
                        wait_data(pool, "ht", phase, k)
                else:
                    pool.wait_ge(xhat_ready, 2 * ph)
                for tt in range(TT):
                    own.then(pool.tensor_tensor(H[:, tt, :], src[:, tt, :], gB[:, :], ALU.mult))
                own.wait()
                for tt in range(TT):
                    own.then(pool.tensor_tensor(H[:, tt, :], H[:, tt, :], bB[:, :], ALU.add))
                own.wait()
                for tt in range(TT):
                    pool.tensor_scalar(H[:, tt, :], H[:, tt, :], ALPHA, None, ALU.mult).then_inc(h_ready, 1)

            def delta(i, j):
                for n in range(8):
                    src = (qT if n < 4 else kT)[:, 2 * (n % 4):2 * (n % 4) + 2, :]
                    pool.wait_ge(silu_qkv, 18 * j + 2 * n + 2)
                    if n >= 2:
                        wait_data(pool, "ss", i, n - 2)
                    pool.tensor_tensor(sq[n % 2].rearrange("p (a b) -> p a b", a=2), src, src, ALU.mult).then_inc(squares, 1)
                pool.wait_ge(gate_silu, j + 1)
                for tt in range(TT):
                    gt = gate[:, tt, :].rearrange("p (h d) -> p h d", h=HEADS)
                    pool.tensor_tensor(gt, gt, angb[:, j, :].unsqueeze(1).to_broadcast([P, HEADS, P]), ALU.mult).then_inc(gate_ready, 1)
                for tt in range(TT):
                    for hg in range(2):
                        pool.wait_ge(egb_ready, 4 * j + 2 * tt + hg + 1)
                        wait_data(pool, "qk", i, tt, hg)
                        sl = qT[:, 4 * hg:4 * hg + 4, tt * P:(tt + 1) * P]
                        pool.tensor_tensor(sl, sl, EGB[:, 4 * hg:4 * hg + 4, :], ALU.mult).then_inc(qdec, 1)

            pool.wait_ge(params_in, N_PARAMS)
            for i, kind in enumerate(kinds):
                j = kinds[:i].count(kind)
                if kind == 0:
                    delta(i, j)
                residual(2 * i + 1, 1, i)
                if with_moe:
                    residual(2 * i + 2, 0, i)

        @block.scalar
        def _(act):
            own = Chain(act, a_chain)
            a = nc.scalar.activation
            act.dma_start(H[:, :, :], w["x"][0].rearrange("(t p) d -> p t d", p=P)).then_inc(x_ready, 16)
            act.dma_start(K_[:, :], w["consts"][:, 0:C_SB]).then_inc(masks_in, 16)
            small = [(onehot, w["consts"][0:REL_BUCKETS + 1, C_OH:C_FLIP])]
            for n, name in enumerate(("ln_mix_g", "ln_mix_b", "ln_ffn_g", "ln_ffn_b")):
                small.append((lnrows[32 * n:32 * n + 32, :], w[name].rearrange("l (k p) -> (l k) p", p=P)))
            for j in range(2):
                small.append((convrows[:, j, :], w["a_conv"][j].rearrange("t (c p) -> (t c) p", p=P)))
                small.append((wab[:, j, :, :], w["a_w_in"][j][:, 4096:4112].rearrange("(k p) n -> p k n", p=P)))
                small.append((alog[:, j, :], bcast(w["a_a_log"][j], HEADS)))
                small.append((dtb[:, j, :], bcast(w["a_dt_bias"][j], HEADS)))
                small.append((angb[:, j, :], bcast(w["a_norm_g"][j], P)))
            small.append((lamb[:, :, :].rearrange("p a b -> p (a b)"), bcast(w["b_lambda"], 256)))
            small.append((bngb[:, :], bcast(w["b_norm_g"], P)))
            small.append((bsrow[:, :], w["c_b_s"][0]))
            small.append((wr[:, :, :], w["w_router"].rearrange("(k p) n -> p k n", p=P)))
            small.append((rbias[:, :], bcast(w["router_bias"], E)))
            assert 16 * (len(small) + 1) == N_PARAMS
            for dst, src in small:
                act.dma_start(dst, src).then_inc(params_in, 16)
            act.wait_ge(consts_set, 4)
            act.dma_start(rel33[0:REL_BUCKETS, :], w["rel_bias"]).then_inc(params_in, 16)

            def ht_chunks(phase):
                for k in range(0, KC, 2):
                    ps = wait_data(act, "ht", phase, k)
                    if phase == 0:
                        emptied(a(HT[:, k, :], ps[:, 0:SEQ], ACT.Copy), "ht", phase, k)
                    else:
                        c = (0 if phase % 2 else 2) * 32 + (phase - 1) // 2 * 8 + k
                        emptied(a(HT[:, k, :], ps[:, 0:SEQ], ACT.Identity, scale=lncols[:, c:c + 1],
                                  bias=lncols[:, c + 32:c + 33]), "ht", phase, k)

            ln_count = 0

            def ahead(func):
                own.link(a(warm[:, :], epsc[:, 0:1], func))

            rsq = 0

            def ln_rstd():
                nonlocal rsq
                rsq += 1
                ahead(ACT.Sqrt)
                act.wait_ge(var_ready, rsq)
                a(rs[:, 0, :], mv[:, :, 1], ACT.Sqrt, bias=epsc[:, 0:1]).then_inc(rstd_ready, 1)

            def heads_norm(nn):
                ahead(ACT.Sqrt)
                act.wait_ge(ss_ready, nn + 1)
                a(ssq[:, 2, :, :], ssq[:, 0, :, :], ACT.Sqrt, bias=epsc[:, 0:1], scale=1.0 / P).then_inc(rms_ready, 1)

            def heads_out_T(i, nn, dst):
                for g in range(0, 4, 2):
                    ps = wait_data(act, "oT", i, g)
                    emptied(a(dst[:, 2 * g:2 * g + 2, :], ps[:, :].rearrange("p (a b) -> p a b", a=2), ACT.Copy), "oT", i, g)

            def delta(i, j):
                emptied(a(abr[:, 0:2, :, :].rearrange("p k t h -> p t k h"),
                          wait_data(act, "ab", i)[:, 0:32].rearrange("p (t k h) -> p t k h", t=TT, k=2), ACT.Copy), "ab", i)
                act.wait_ge(ab_mid, 2 * j + 1)
                own.link(a(abr[:, 4, :, :], abr[:, 3, :, :], ACT.Exp, scale=-1.0))
                own.then(a(abr[:, 5, :, :], abr[:, 1, :, :], ACT.Exp, scale=-1.0))
                own.then(a(abr[:, 4, :, :], abr[:, 4, :, :], ACT.Ln, bias=1.0))
                a(gsc[:, 7, 0, :], alog[:, j, :], ACT.Exp).then_inc(ab_exp, 1)

                def silu(c):
                    wait_copy(act, "conv", i, c)
                    dst = (qT, kT)[c // 8][:, c % 8, :]
                    a(dst, cv[c % 4], ACT.Silu).then_inc(silu_qkv, 1)

                def tap(c):
                    ps = wait_data(act, "conv", i, c)
                    if c < 16:
                        if c >= 4:
                            act.wait_ge(silu_qkv, 18 * j + c - 3)
                        dst = cv[c % 4]
                    else:
                        dst = vT[:, c - 16, :]
                    a(dst, ps[:, 0:SEQ], ACT.Copy, scale=convcols[:, j, 72 + c:73 + c]).then_inc(tap_ready, 1)

                for c in range(17):
                    tap(c) if c < 16 else None
                    if c >= 1:
                        silu(c - 1)
                for c in range(16, 24):
                    tap(c)
                    n = c - 16
                    ps = wait_data(act, "ss", i, n)
                    if n >= 2:
                        act.wait_ge(qk_normed, 8 * j + n - 1)
                    emptied(a(lnr[n % 2], ps[:, :], ACT.Ln, bias=epsc[:, 1:2]), "ss", i, n)
                    wait_copy(act, "ss", i, n)
                    a(lnr[n % 2], lnr[n % 2], ACT.Exp, scale=-0.5).then_inc(rnorm, 1)
                for nh in range(2):
                    for tt in range(TT):
                        emptied(a(gate[:, tt, nh * 512:(nh + 1) * 512], wait_data(act, "gate", i, tt, nh)[:, :], ACT.Copy), "gate", i, tt, nh)
                for c in range(16, 24):
                    wait_copy(act, "conv", i, c)
                for n in range(2):
                    a(vT[:, 4 * n:4 * n + 4, :], vT[:, 4 * n:4 * n + 4, :], ACT.Silu).then_inc(silu_qkv, 1)
                for nh in range(2):
                    for tt in range(TT):
                        wait_copy(act, "gate", i, tt, nh)
                a(gate[:, :, :], gate[:, :, :], ACT.Silu).then_inc(gate_silu, 1)
                act.wait_ge(gcol_ready, j + 1)
                own.then(a(gsc[:, 4, :, :], gsc[:, 0, :, :], ACT.Exp))
                a(gsc[:, 5, :, :], gsc[:, 3, :, :], ACT.Exp).then_inc(gexp, 1)
                for tt in range(TT):
                    for hg in range(2):
                        ps = wait_data(act, "GB", i, tt, hg)
                        if tt:
                            wait_data(act, "su", i, 0, 1, hg)
                        a(EGB[:, 4 * hg:4 * hg + 4, :], ps[:, :].rearrange("p (a b) -> p a b", a=4), ACT.Exp).then_inc(egb_ready, 1)
                    for hg in range(2):
                        wait_copy(act, "GB", i, tt, hg)
                        for h in range(4 * hg, 4 * hg + 4):
                            ins = a(DT[:, h, :], DT[:, h, :], ACT.Exp, bias=gsc[:, 2, tt, h:h + 1])
                        ins.then_inc(decay, 1)
                    for hg in range(2):
                        for key, dst in (("Ktok", Ktok), ("Vtok", Vtok)):
                            ps = wait_data(act, key, i, tt, hg)
                            if tt and key == "Vtok":
                                wait_data(act, "vn", i, 0, 0, hg)
                            emptied(a(dst[:, 4 * hg:4 * hg + 4, :], ps[:, :].rearrange("p (a b) -> p a b", a=4), ACT.Copy), key, i, tt, hg)
                    for hg in range(2):
                        ps = wait_data(act, "T0", i, tt, hg)
                        if tt:
                            wait_data(act, "vn", i, 0, 1, hg)
                        emptied(a(T[:, 4 * hg:4 * hg + 4, :], ps[:, :].rearrange("p (a b) -> p a b", a=4), ACT.Copy), "T0", i, tt, hg)
                    for lv in range(1, LEVELS):
                        for hg in range(2):
                            ps = wait_data(act, "Y", i, tt, lv, hg)
                            if lv == 1:
                                act.wait_ge(qdec, 4 * j + 2 * tt + hg + 1)
                            else:
                                wait_data(act, "T", i, tt, lv - 1, hg)
                            emptied(a(Y[:, 4 * hg:4 * hg + 4, :], ps[:, :].rearrange("p (a b) -> p a b", a=4), ACT.Copy), "Y", i, tt, lv, hg)
                    for hg in range(2):
                        wait_data(act, "TT", i, tt, LEVELS - 1, hg)
                        for h in range(4 * hg, 4 * hg + 4):
                            ins = a(kG[:, h, :], Ktok[:, h, :], ACT.Copy, scale=gsc[:, 4, tt, h:h + 1])
                        ins.then_inc(kscaled, 1)
                    for hg in range(2):
                        ps = wait_data(act, "W", i, tt, hg)
                        emptied(a(NWT[:, 4 * hg:4 * hg + 4, :], ps[:, :].rearrange("p (a b) -> p a b", a=4), ACT.Copy, scale=-1.0), "W", i, tt, hg)
                    for hg in range(2):
                        for h in range(4 * hg, 4 * hg + 4):
                            ins = a(kd[:, h, :], Ktok[:, h, :], ACT.Copy, scale=gsc[:, 5, tt, h:h + 1])
                        ins.then_inc(kd_ready, 1)
                    for hg in range(2):
                        ps = wait_data(act, "o", i, tt, hg)
                        emptied(a(O[:, 4 * hg:4 * hg + 4, tt * P:(tt + 1) * P], ps[:, :].rearrange("p (a b) -> p a b", a=4), ACT.Copy), "o", i, tt, hg)

            def attention(i, j):
                if j == 0:
                    act.wait_ge(lam_dot, 1)
                    a(lm[:, 2:4], lm[:, 0:2], ACT.Exp).then_inc(lam_exp, 1)
                act.wait_ge(rel_out, 16)
                for k in range(KC):
                    wait_data(act, "ht", 2 * i, k)
                act.dma_start(flip, w["consts"][:, C_FLIP:C_ALL]).then_inc(toep_in, 16)
                for lo, n, off in ((0, P, P), (P, SEQ, 0)):
                    act.dma_start(TBr.rearrange("p (h k) -> p h k", h=HEADS)[:, :, lo:lo + n],
                                  bass.AP(tensor=scratch.tensor, offset=off, ap=[[1, P], [TOEP, HEADS], [1, n]])).then_inc(toep_in, 16)
                for c in range(16):
                    ps = wait_data(act, "qkT", i, c)
                    emptied(a((qT, kT)[c // 8][:, c % 8, :], ps[:, 0:SEQ], ACT.Copy, scale=0.125 if c < 8 else 1.0), "qkT", i, c)
                for nh in range(2):
                    for tt in range(TT):
                        emptied(a(Vb[:, tt, nh * 512:(nh + 1) * 512], wait_data(act, "v", i, tt, nh)[:, :], ACT.Copy), "v", i, tt, nh)
                for h in range(HEADS + 2):
                    if h < HEADS:
                        act.wait_ge(nmax, HEADS * j + h + 1)
                        for m in range(2):
                            a(L[h % 2][:, m, 0:P], L[h % 2][:, m, 0:P], ACT.Exp, bias=sm[:, h, m:m + 1], accum_out=sm[:, h, 4 + m:5 + m])
                            ins = a(L[h % 2][:, m, P:TOEP], L[h % 2][:, m, P:TOEP], ACT.Exp, bias=sm[:, h, 2 + m:3 + m], accum_out=sm[:, h, 6 + m:7 + m])
                        ins.then_inc(probs, 1)
                    if 1 <= h <= HEADS:
                        ps = wait_data(act, "pT", i, h - 1)
                        if h - 1 >= 2:
                            wait_data(act, "ob", i, h - 3)
                        emptied(a(PT[(h - 1) % 2], ps[:, 0:TOEP], ACT.Copy), "pT", i, h - 1)
                    if h >= 2:
                        g = h - 2
                        emptied(a(bO[:, g, :], wait_data(act, "ob", i, g)[:, 0:SEQ], ACT.Copy), "ob", i, g)

            def gmlp(i, j):
                for k in range(KC):
                    wait_data(act, "ht", 2 * i, k)
                act.dma_start(gC, bcast(w["c_ln_g"][j], 2048)).then_inc(cpar_in, 16)
                act.dma_start(bC, bcast(w["c_ln_b"][j], 2048)).then_inc(cpar_in, 16)
                act.dma_start(ws, w["c_w_s"][j].rearrange("g t s -> t g s")).then_inc(cpar_in, 16)
                for u in (4, 5, 6, 7, 0, 1, 2, 3):
                    for tt in range(TT):
                        ps = wait_data(act, "z", i, u, tt)
                        dst = v_[:, tt, (u - 4) * 512:(u - 3) * 512] if u >= 4 else u_[:, tt, u * 512:(u + 1) * 512]
                        emptied(a(dst, ps[:, :], ACT.Gelu), "z", i, u, tt)
                    if u == 7:
                        ln_rstd()
                for g in range(0, 8, 2):
                    ps = wait_data(act, "uT", i, g)
                    emptied(a(uT[:, 2 * g:2 * g + 2, :], ps[:, :].rearrange("p (a b) -> p a b", a=2), ACT.Copy), "uT", i, g)

            def experts(i):
                ahead(ACT.Exp)
                emptied(a(rt[:, 0, :], wait_data(act, "rt", i)[:, 0:TT * E], ACT.Exp, scale=-1.0), "rt", i)
                wait_copy(act, "rank", i)
                first = at[("moe", i)]
                with act.Fori(0, E // 2) as it:
                    for j in range(2):
                        count = act.value_load(counts[0:1, bass.ds(it * 2 + j, 1)], min_val=0, max_val=SEQ)
                        act.wait_ge(filled[2], it * 4 + (first[2] + 2 * j + 1))
                        a(sil[CAP:, :], bank[2][0:CAP, :], ACT.Silu).then_inc(silu_h, 1)
                        for n in range(1, PASSES):
                            with act.If(count > CAP * n):
                                b0 = act.snap(steps_done)
                                act.wait_ge(baton, b0 + 5)
                                a(m_sil[CAP:, :], bank[5][0:CAP, :], ACT.Silu).then_inc(baton, 1)
                                act.reg_add(steps_done, steps_done, H_STEPS)
                        act.wait_ge(filled[2], it * 4 + (first[2] + 2 * j + 2))
                        a(selgT[:, j * P:(j + 1) * P], bank[2][:, 0:P], ACT.Copy)
                        a(hT, bank[2][:, SEQ:].rearrange("p (m c) -> p m c", m=4), ACT.Copy).then_inc(drained[2], 1)
                        for n in range(1, PASSES):
                            with act.If(count > CAP * n):
                                b0 = act.snap(steps_done)
                                act.wait_ge(baton, b0 + 1)
                                a(m_turned, bank[6][:, :], ACT.Copy).then_inc(baton, 1)
                                act.wait_ge(baton, b0 + 3)
                                a(m_y, bank[7][:, :], ACT.Copy).then_inc(baton, 1)
                                act.reg_add(steps_done, steps_done, Y_STEPS)
                        act.wait_ge(filled[3], it * 2 + (first[3] + j + 1))
                        for nh in range(2):
                            ins = a(y_[CAP * j:CAP * (j + 1), nh * 512:(nh + 1) * 512], bank[3][nh * CAP:(nh + 1) * CAP, :], ACT.Copy)
                        ins.then_inc(drained[3], 1)

            steps_done = act.alloc_register("steps_done_act")
            act.reg_mov(steps_done, 1)
            ht_chunks(0)
            act.wait_ge(params_in, N_PARAMS)
            emptied(a(relrow[:, :], wait_data(act, "relrow")[0:HEADS, 0:TOEP], ACT.Copy), "relrow")
            wait_copy(act, "relrow")
            act.dma_start(scratch, relrow[:, :]).then_inc(rel_out, 16)
            nn = 0
            for i, kind in enumerate(kinds):
                j = kinds[:i].count(kind)
                if kind == 0:
                    delta(i, j)
                    heads_norm(nn)
                    heads_out_T(i, nn, OT)
                    nn += 1
                elif kind == 1:
                    attention(i, j)
                    heads_norm(nn)
                    heads_out_T(i, nn, bOT)
                    nn += 1
                else:
                    gmlp(i, j)
                ln_rstd()
                if 2 * i + 1 != last_phase:
                    ht_chunks(2 * i + 1)
                if with_moe:
                    experts(i)
                    ln_rstd()
                if i < n_layers - 1:
                    ht_chunks(2 * i + 2)

        @block.vector
        def _(dve):
            v = nc.vector
            own = Chain(dve, v_chain)

            def ht_chunks(phase):
                for k in range(1, KC, 2):
                    ps = wait_data(dve, "ht", phase, k)
                    if phase == 0:
                        emptied(v.tensor_copy(HT[:, k, :], ps[:, 0:SEQ]), "ht", phase, k)
                    else:
                        c = (0 if phase % 2 else 2) * 32 + (phase - 1) // 2 * 8 + k
                        emptied(v.tensor_scalar(HT[:, k, :], ps[:, 0:SEQ], lncols[:, c:c + 1], lncols[:, c + 32:c + 33],
                                                ALU.mult, ALU.add), "ht", phase, k)

            rsq = 0
            lnn = 0

            def block_stats(X, tt, b):
                own.then(v.bn_stats(stats[:, tt, 6 * b:6 * b + 6], X[:, tt, b * 512:(b + 1) * 512]))

            def rstd(blocks):
                nonlocal rsq
                own.wait()
                for tt in range(TT):
                    ins = v.bn_aggr(mv[:, tt, :], stats[:, tt, 0:6 * blocks])
                    if tt < TT - 1:
                        own.then(ins)
                rsq += 1
                ins.then_inc(var_ready, 1)
                dve.wait_ge(rstd_ready, rsq)
                own.link(v.reciprocal(rs[:, 0, :], rs[:, 0, :]))
                own.link(v.tensor_tensor(rs[:, 1, :], rs[:, 0, :], rs[:, 0, :], ALU.mult))
                own.link(v.scalar_tensor_tensor(rs[:, 2, :], mv[:, :, 1], EPS, rs[:, 1, :], ALU.add, ALU.mult))
                own.link(v.tensor_scalar(rs[:, 1, :], rs[:, 2, :], -0.5, 1.5, ALU.mult, ALU.add))
                own.link(v.tensor_tensor(rs[:, 3, :], rs[:, 1, :], rs[:, 0, :], ALU.mult))

            def layer_norm(phase):
                nonlocal lnn
                rstd(2)
                lnn += 1
                if phase == last_phase:
                    dve.wait_ge(rows_in, 32 * len(phases))
                    for tt in range(TT):
                        own.then(v.scalar_tensor_tensor(H[:, tt, :], H[:, tt, :], mv[:, tt, 0:1], gB[:, :], ALU.subtract, ALU.mult))
                        own.wait()
                        v.scalar_tensor_tensor(H[:, tt, :], H[:, tt, :], rs[:, 3, tt:tt + 1], bB[:, :], ALU.mult, ALU.add).then_inc(h_ready, 1)
                    return
                dst = XH if phase % 2 else H
                for tt in range(TT):
                    v.tensor_scalar(dst[:, tt, :], H[:, tt, :], mv[:, tt, 0:1], rs[:, 3, tt:tt + 1],
                                    ALU.subtract, ALU.mult).then_inc(xhat_ready, 1)

            def add_mixed(i):
                for nh in range(2):
                    for tt in range(TT):
                        ps = wait_data(dve, "y", i, tt, nh)
                        sl = H[:, tt, nh * 512:(nh + 1) * 512]
                        emptied(v.tensor_tensor(sl, ps[:, :], sl, ALU.add), "y", i, tt, nh)
                    for tt in range(TT):
                        wait_copy(dve, "y", i, tt, nh)
                        block_stats(H, tt, nh)

            def heads_norm(nn, X, gain, scale):
                for tt in range(TT):
                    own.wait()
                    own.link(v.tensor_tensor(X2, X(tt), X(tt), ALU.mult))
                    ins = v.tensor_reduce(ssq[:, 0, tt, :], X2, AX, ALU.add)
                    own.then(ins) if tt < TT - 1 else ins.then_inc(ss_ready, 1)
                for tt in range(TT):
                    own.then(v.tensor_tensor(X(tt), X(tt), gain(tt), ALU.mult))
                dve.wait_ge(rms_ready, nn + 1)
                own.link(v.reciprocal(ssq[:, 1, :, :], ssq[:, 2, :, :]))
                own.link(v.tensor_scalar(ssq[:, 3, :, :], ssq[:, 1, :, :], scale, None, ALU.mult))
                for tt in range(TT):
                    v.tensor_tensor(X(tt), X(tt), ssq[:, 3, tt, :].unsqueeze(2).to_broadcast([P, HEADS, P]), ALU.mult).then_inc(o_ready, 1)

            def heads_out_T(i, nn, dst):
                for g in range(1, 4, 2):
                    ps = wait_data(dve, "oT", i, g)
                    emptied(v.tensor_copy(dst[:, 2 * g:2 * g + 2, :], ps[:, :].rearrange("p (a b) -> p a b", a=2)), "oT", i, g)

            def delta(i, j):
                wait_copy(dve, "ab", i)
                own.link(v.tensor_tensor(abr[:, 2, :, :], abr[:, 0, :, :], dtb[:, j, :].unsqueeze(1).to_broadcast([P, TT, HEADS]), ALU.add))
                own.link(v.tensor_scalar(abr[:, 3, :, :], abr[:, 2, :, :], -1.0, None, ALU.mult))
                v.tensor_tensor(abr[:, 3, :, :], abr[:, 2, :, :], abr[:, 3, :, :], ALU.max).then_inc(ab_mid, 1)
                dve.wait_ge(ab_exp, j + 1)
                own.link(v.tensor_scalar(abr[:, 5, :, :], abr[:, 5, :, :], 1.0, None, ALU.add))
                own.then(v.reciprocal(gsc[:, 6, :, :], abr[:, 5, :, :]))
                own.link(v.scalar_tensor_tensor(abr[:, 6, :, :], abr[:, 2, :, :], 0.0, abr[:, 4, :, :], ALU.max, ALU.add))
                own.link(v.tensor_scalar(abr[:, 6, :, :], abr[:, 6, :, :], -1.0, None, ALU.mult))
                v.tensor_tensor(abr[:, 7, :, :], abr[:, 6, :, :], gsc[:, 7, 0, :].unsqueeze(1).to_broadcast([P, TT, HEADS]), ALU.mult).then_inc(ab_mid, 1)

                def conv(c):
                    ps = wait_data(dve, "conv", i, c)
                    dve.wait_ge(tap_ready, 24 * j + c + 1)
                    dst = cv[c % 4] if c < 16 else vT[:, c - 16, :]
                    for back in (1, 2, 3):
                        col = 24 * (3 - back) + c
                        ins = v.scalar_tensor_tensor(dst[:, back:SEQ], ps[:, 0:SEQ - back], convcols[:, j, col:col + 1],
                                                     dst[:, back:SEQ], ALU.mult, ALU.add)
                        if back < 3:
                            own.link(ins)
                    emptied(ins, "conv", i, c)

                def normed(n):
                    dve.wait_ge(rnorm, 8 * j + n + 1)
                    dst = (qT if n < 4 else kT)[:, 2 * (n % 4):2 * (n % 4) + 2, :]
                    sc = float(P) ** -0.5 if n < 4 else 1.0
                    v.scalar_tensor_tensor(dst, dst, sc, lnr[n % 2].rearrange("p (a b) -> p a b", a=2), ALU.mult, ALU.mult).then_inc(qk_normed, 1)

                for c in range(24):
                    conv(c)
                    if c >= 17:
                        normed(c - 17)
                normed(7)
                ps = wait_data(dve, "G", i)
                own.then(v.tensor_copy(gsc[:, 0:2, :, :], ps[:, 0:32].rearrange("p (k t h) -> p k t h", k=2, t=TT)))
                own.wait()
                emptied(v.tensor_scalar(gsc[:, 2, :, :], ps[:, 0:16].rearrange("p (t h) -> p t h", t=TT), -1.0, None, ALU.mult), "G", i)
                v.tensor_tensor(gsc[:, 3, :, :], gsc[:, 1, :, :], gsc[:, 0, :, :], ALU.subtract).then_inc(gcol_ready, 1)
                own.then(v.memset(S[:, :, :], 0.0))
                for tt in range(TT):
                    for hg in range(2):
                        hs = slice(4 * hg, 4 * hg + 4)
                        ps = wait_data(dve, "GB", i, tt, hg)
                        dve.wait_ge(egb_ready, 4 * j + 2 * tt + hg + 1)
                        if tt:
                            wait_data(dve, "o", i, 0, hg)
                        g4 = ps[:, :].rearrange("p (a b) -> p a b", a=4)
                        own.then(v.tensor_tensor(DT[:, hs, :], g4, neg_mask.unsqueeze(1).to_broadcast([P, 4, P]), ALU.add))
                        own.wait()
                        if hg == 0 and tt:
                            dve.wait_ge(s_scaled, 6 * j + 4)
                        emptied(v.tensor_copy(egl[:, hs, :], EGB[:, hs, 63:128:64]), "GB", i, tt, hg)
                    for hg in range(2):
                        hs = slice(4 * hg, 4 * hg + 4)
                        dve.wait_ge(decay, 4 * j + 2 * tt + hg + 1)
                        ps = wait_data(dve, "kk", i, tt, hg)
                        for h in range(4 * hg, 4 * hg + 4):
                            ins = v.scalar_tensor_tensor(AT[:, h, :], ps[:, (h % 4) * P:(h % 4 + 1) * P], gsc[:, 6, tt, h:h + 1],
                                                         DT[:, h, :], ALU.mult, ALU.mult)
                        emptied(ins, "kk", i, tt, hg)
                        ps = wait_data(dve, "qk", i, tt, hg)
                        if tt:
                            wait_data(dve, "o", i, 0, hg)
                        emptied(v.tensor_tensor(attnT[:, hs, :], ps[:, :].rearrange("p (a b) -> p a b", a=4), DT[:, hs, :], ALU.mult), "qk", i, tt, hg)
                    for hg in range(2):
                        hs = slice(4 * hg, 4 * hg + 4)
                        wait_copy(dve, "kk", i, tt, hg)
                        if tt:
                            wait_data(dve, "vn", i, 0, 1, hg)
                            wait_data(dve, "W", i, 0, hg)
                        own.link(v.tensor_tensor(AM[:, hs, :], AT[:, hs, :], level(0).unsqueeze(1).to_broadcast([P, 4, P]), ALU.mult))
                        v.scalar_tensor_tensor(Ti[:, hs, :], AM[:, hs, :], -1.0, ident.unsqueeze(1).to_broadcast([P, 4, P]),
                                               ALU.mult, ALU.add).then_inc(inv_done, 1)
                    def mask(lv):
                        for hg in range(2):
                            hs = slice(4 * hg, 4 * hg + 4)
                            if lv == 1:
                                dve.wait_ge(inv_done, 4 * j + 2 * tt + hg + 1)
                            else:
                                wait_data(dve, "Y", i, tt, lv - 1, hg)
                            v.tensor_tensor(AM[:, hs, :], AT[:, hs, :], level(lv).unsqueeze(1).to_broadcast([P, 4, P]), ALU.mult).then_inc(masked, 1)

                    mask(1)
                    for lv in range(1, LEVELS):
                        if lv < LEVELS - 1:
                            mask(lv + 1)
                        for hg in range(2):
                            hs = slice(4 * hg, 4 * hg + 4)
                            psT = wait_data(dve, "TT", i, tt, lv, hg)
                            if lv < LEVELS - 1:
                                psU = wait_data(dve, "T", i, tt, lv, hg)
                            if lv > 1:
                                wait_copy(dve, "TT", i, tt, lv - 1, hg)
                                wait_copy(dve, "T", i, tt, lv - 1, hg)
                            emptied(v.tensor_tensor(Ti[:, hs, :], Ti[:, hs, :], psT[:, :].rearrange("p (a b) -> p a b", a=4), ALU.subtract), "TT", i, tt, lv, hg)
                            if lv < LEVELS - 1:
                                emptied(v.tensor_tensor(T[:, hs, :], T[:, hs, :], psU[:, :].rearrange("p (a b) -> p a b", a=4), ALU.subtract), "T", i, tt, lv, hg)
                    for c in range(2):
                        r0 = slice(64 * c, 64 * c + 64)
                        last = (tt, c) == (TT - 1, 1)
                        for hg in range(2):
                            hs = slice(4 * hg, 4 * hg + 4)
                            ps = wait_data(dve, "vn", i, tt, c, hg)
                            emptied(v.tensor_tensor(vnew[r0, hs, :], ps[r0, :].rearrange("p (a b) -> p a b", a=4),
                                                    gsc[r0, 6, tt, hs].unsqueeze(2).to_broadcast([64, 4, P]), ALU.mult), "vn", i, tt, c, hg)
                            if not last:
                                v.tensor_tensor(S[:, hs, :], S[:, hs, :], egl[:, hs, c:c + 1].to_broadcast([P, 4, P]), ALU.mult).then_inc(s_scaled, 1)
                        if last:
                            continue
                        for hg in range(2):
                            hs = slice(4 * hg, 4 * hg + 4)
                            ps = wait_data(dve, "su", i, tt, c, hg)[:, :].rearrange("p (a b) -> p a b", a=4)
                            dve.wait_ge(s_scaled, 6 * j + 2 * (2 * tt + c) + hg + 1)
                            emptied(v.tensor_tensor(S[:, hs, :], ps, S[:, hs, :], ALU.add), "su", i, tt, c, hg)
                for tt in range(TT):
                    for hg in range(2):
                        wait_copy(dve, "o", i, tt, hg)
                dve.wait_ge(gate_ready, 2 * j + 2)

            def level(lv):
                return K_[:, C_LV + lv * P:C_LV + (lv + 1) * P]

            def attention(i, j, lam_init):
                if j == 0:
                    own.link(v.tensor_tensor(lamb[:, 0:4:2, :], lamb[:, 0:4:2, :], lamb[:, 1:4:2, :], ALU.mult))
                    v.tensor_reduce(lm[:, 0:2], lamb[:, 0:4:2, :], AX, ALU.add).then_inc(lam_dot, 1)
                    dve.wait_ge(lam_exp, 1)
                    own.link(v.tensor_tensor(lm[:, 4:5], lm[:, 3:4], lm[:, 2:3], ALU.subtract))
                    own.link(v.tensor_scalar(lm[:, 5:6], lm[:, 4:5], -lam_init, None, ALU.add))
                for n in range(6):
                    ps = wait_data(dve, "flip", i, n)
                    emptied(v.tensor_copy(work[:, 8192 + n * 512:8192 + (n + 1) * 512], ps[:, :]), "flip", i, n)
                for n in range(6):
                    wait_copy(dve, "flip", i, n)
                for h in range(HEADS + 1):
                    if h < HEADS:
                        Lh = L[h % 2]
                        if h >= 2:
                            dve.wait_ge(pa_ready, HEADS * j + h - 1)
                        for m in range(2):
                            ps = wait_data(dve, "lg", i, h, m)
                            emptied(v.tensor_tensor(Lh[:, m, :], ps[:, 0:TOEP], TB[:, h, :], ALU.add), "lg", i, h, m)
                        wait_copy(dve, "lg", i, h, 0)
                        wait_copy(dve, "lg", i, h, 1)
                        own.then(v.tensor_reduce(sm[:, h, 0:2], Lh[:, :, 0:P], AX, ALU.max))
                        own.link(v.tensor_reduce(sm[:, h, 2:4], Lh[:, :, P:TOEP], AX, ALU.max))
                        v.tensor_scalar(sm[:, h, 0:4], sm[:, h, 0:4], -1.0, None, ALU.mult).then_inc(nmax, 1)
                    if h >= 1:
                        g = h - 1
                        Lg, A = L[g % 2], PA[g % 2]
                        dve.wait_ge(probs, HEADS * j + g + 1)
                        own.link(v.reciprocal(sm[:, g, 4:8], sm[:, g, 4:8]))
                        own.link(v.tensor_scalar(sm[:, g, 5:8:2], sm[:, g, 5:8:2], lm[:, 5:6], None, ALU.mult))
                        if g >= 2:
                            wait_data(dve, "pT", i, g - 2)
                        own.then(v.tensor_scalar(A[:, 0:P], Lg[:, 0, 0:P], sm[:, g, 4:5], None, ALU.mult))
                        own.link(v.tensor_scalar(A[:, P:TOEP], Lg[:, 0, P:TOEP], sm[:, g, 6:7], None, ALU.mult))
                        own.then(v.scalar_tensor_tensor(A[:, 0:P], Lg[:, 1, 0:P], sm[:, g, 5:6], A[:, 0:P], ALU.mult, ALU.add))
                        v.scalar_tensor_tensor(A[:, P:TOEP], Lg[:, 1, P:TOEP], sm[:, g, 7:8], A[:, P:TOEP], ALU.mult, ALU.add).then_inc(pa_ready, 1)
                for h in range(HEADS):
                    wait_copy(dve, "ob", i, h)

            def gmlp(i, j):
                for b in range(4):
                    for tt in range(TT):
                        wait_copy(dve, "z", i, 4 + b, tt)
                        block_stats(v_, tt, b)
                dve.wait_ge(cpar_in, 48)
                for g in range(2):
                    ps = wait_data(dve, "wsT", i, g)
                    emptied(v.tensor_tensor(wsT[:, 4 * g:4 * g + 4, :], ps[:, :].rearrange("p (a b) -> p a b", a=4),
                                            tri.unsqueeze(1).to_broadcast([P, 4, P]), ALU.mult), "wsT", i, g)
                rstd(4)
                for tt in range(TT):
                    own.link(v.scalar_tensor_tensor(v_[:, tt, :], v_[:, tt, :], mv[:, tt, 0:1], gC, ALU.subtract, ALU.mult))
                    v.scalar_tensor_tensor(v_[:, tt, :], v_[:, tt, :], rs[:, 3, tt:tt + 1], bC, ALU.mult, ALU.add).then_inc(v_ln, 1)
                for tt in range(TT):
                    for g2 in range(4):
                        wait_copy(dve, "z", i, g2, tt)
                        ps = wait_data(dve, "mix", i, tt, g2)
                        for g in (2 * g2, 2 * g2 + 1):
                            sl = u_[:, tt, g * 256:(g + 1) * 256]
                            ins = v.scalar_tensor_tensor(sl, ps[:, (g % 2) * 256:(g % 2 + 1) * 256], bscol[:, g:g + 1], sl, ALU.add, ALU.mult)
                        emptied(ins, "mix", i, tt, g2)
                for g in range(1, 8, 2):
                    ps = wait_data(dve, "uT", i, g)
                    emptied(v.tensor_copy(uT[:, 2 * g:2 * g + 2, :], ps[:, :].rearrange("p (a b) -> p a b", a=2)), "uT", i, g)

            def route(i):
                wait_copy(dve, "rt", i)
                R = [rt[:, n, :] for n in range(8)]
                V3 = lambda n: rt[:, n, :].rearrange("p (t e) -> p t e", t=TT)
                G4 = lambda n: rt[:, n, :].rearrange("p (a e) -> p a e", e=4)
                own.link(v.tensor_scalar(R[1], R[0], 1.0, None, ALU.add))
                own.link(v.reciprocal(R[1], R[1]))
                own.link(v.tensor_tensor(V3(2), V3(1), rbias[:, :].unsqueeze(1).to_broadcast([P, TT, E]), ALU.add))
                g = [rg[:, n, :] for n in range(8)]
                s = G4(2)
                own.then(v.tensor_tensor(g[0], s[:, :, 0], s[:, :, 1], ALU.max))
                own.then(v.tensor_tensor(g[1], s[:, :, 0], s[:, :, 1], ALU.min))
                own.then(v.tensor_tensor(g[2], s[:, :, 2], s[:, :, 3], ALU.max))
                own.link(v.tensor_tensor(g[3], s[:, :, 2], s[:, :, 3], ALU.min))
                own.then(v.tensor_tensor(g[4], g[0], g[2], ALU.max))
                own.then(v.tensor_tensor(g[5], g[0], g[2], ALU.min))
                own.link(v.tensor_tensor(g[6], g[1], g[3], ALU.max))
                own.link(v.tensor_tensor(g[5], g[5], g[6], ALU.max))
                own.link(v.tensor_tensor(g[4], g[4], g[5], ALU.add))

                def first_max(x, size, pre, wts, outp, mx):
                    x3 = x.rearrange("p (t e) -> p t e", t=TT)
                    o3 = outp.rearrange("p (t e) -> p t e", t=TT)
                    w3 = wts.rearrange("p (t e) -> p t e", t=TT)
                    own.link(v.tensor_reduce(mx, x3, AX, ALU.max))
                    own.link(v.tensor_tensor(w3, x3, mx.unsqueeze(2).to_broadcast([P, TT, size]), ALU.is_equal))
                    own.link(v.tensor_tensor(w3, w3, pre.unsqueeze(1).to_broadcast([P, TT, size]), ALU.mult))
                    own.link(v.tensor_reduce(mx, w3, AX, ALU.max))
                    own.link(v.tensor_tensor(o3, w3, mx.unsqueeze(2).to_broadcast([P, TT, size]), ALU.is_equal))

                countdown = K_[:, C_CD:C_CD + E]
                first_max(g[4], GROUPS, countdown[:, E - GROUPS:E], g[5], g[6], rs[:, 1, :])
                own.link(v.tensor_scalar(g[7], g[6], BIG, -BIG, ALU.mult, ALU.add))
                own.link(v.tensor_tensor(G4(3), s, g[6].unsqueeze(2).to_broadcast([P, TT * GROUPS, 4]), ALU.mult))
                own.link(v.tensor_tensor(G4(3), G4(3), g[7].unsqueeze(2).to_broadcast([P, TT * GROUPS, 4]), ALU.add))
                first_max(R[3], E, countdown, R[4], R[5], rs[:, 1, :])
                own.link(v.scalar_tensor_tensor(R[3], R[5], -BIG, R[3], ALU.mult, ALU.add))
                first_max(R[3], E, countdown, R[4], R[6], rs[:, 1, :])
                v.tensor_tensor(R[7], R[5], R[6], ALU.add).then_inc(mask_ready, 1)
                dve.wait_ge(mask_ready, i + 1)
                own.link(v.tensor_tensor(R[5], R[7], R[1], ALU.mult))
                own.link(v.tensor_reduce(rs[:, 1, :], V3(5), AX, ALU.add))
                own.link(v.reciprocal(rs[:, 2, :], rs[:, 1, :]))
                own.link(v.tensor_tensor(gates[:, :, :], V3(5), rs[:, 2, :].unsqueeze(2).to_broadcast([P, TT, E]), ALU.mult))

            def rank(i):
                ps = wait_data(dve, "rank", i)
                v.tensor_copy(counts[0:1, :], ps[0:1, 2 * E:3 * E])
                p0 = place[:, :, 0:E]
                own.link(v.tensor_tensor(p0, ps[:, 0:TT * E].rearrange("p (t e) -> p t e", t=TT),
                                         rt[:, 7, :].rearrange("p (t e) -> p t e", t=TT), ALU.mult))
                for n in range(PASSES - 1, -1, -1):
                    ins = v.tensor_scalar(place[:, :, n * (E + 2):n * (E + 2) + E], p0, -1.0 - CAP * n, None, ALU.add)
                    if n:
                        own.then(ins)
                emptied(ins, "rank", i)
                wait_copy(dve, "rank", i)

            def experts(i, nres):
                route(i)
                rank(i)
                first = at[("moe", i)]
                def columns(first_col, cap):
                    return lncols[:, first_col:first_col + KC].unsqueeze(2).to_broadcast([P, KC, cap])

                g_col, b_col = KC * i, 32 + KC * i
                iota = iota2[:, 0:CAP]

                def part(b):
                    tt, nh = (b - 4) // 2, (b - 4) % 2
                    return H[:, tt, nh * 512:(nh + 1) * 512]

                def pair_x(g):
                    sl = x_[:, 4 * g:4 * g + 4, :]
                    v.tensor_tensor(sl, bank[g][:, :].rearrange("p (k c) -> p k c", k=4),
                                    lncols[:, g_col + 4 * g:g_col + 4 * g + 4].unsqueeze(2).to_broadcast([P, 4, 2 * CAP]), ALU.mult).then_inc(x_scaled, 1)

                def pair_x_shift(g):
                    sl = x_[:, 4 * g:4 * g + 4, :]
                    v.tensor_tensor(sl, sl, lncols[:, b_col + 4 * g:b_col + 4 * g + 4].unsqueeze(2).to_broadcast([P, 4, 2 * CAP]),
                                    ALU.add).then_inc(drained[g], 1)

                for tt in range(TT):
                    for j in range(2):
                        ins = v.tensor_scalar(sel[:, tt, CAP * j:CAP * (j + 1)], iota, place[:, tt, j:j + 1], None, ALU.is_equal)
                ins.then_inc(sel_ready, 1)
                for g in range(2):
                    wait_data(dve, "first", i, g)
                    pair_x(g)
                for g in range(2):
                    dve.wait_ge(x_scaled, (E + 2) * i + g + 1)
                    pair_x_shift(g)
                dve.wait_ge(h_ready, 2 * nres)
                with dve.Fori(0, E // 2) as it:
                    for tt in range(TT):
                        for j in range(2):
                            v.tensor_scalar(selg[:, tt, CAP * j:CAP * (j + 1)], iota, place[:, tt, bass.ds(it * 2 + j, 1)],
                                            gates[:, tt, bass.ds(it * 2 + j, 1)], ALU.is_equal, ALU.mult)
                            ins = v.tensor_scalar(sel[:, tt, CAP * j:CAP * (j + 1)], iota, place[:, tt, bass.ds(it * 2 + (j + 2), 1)], None, ALU.is_equal)
                    ins.then_inc(sel_ready, 1)
                    for j in range(2):
                        count = dve.value_load(counts[0:1, bass.ds(it * 2 + j, 1)], min_val=0, max_val=SEQ)
                        dve.wait_ge(silu_h, it * 2 + (E * i + j + 1))
                        v.tensor_tensor(h_[CAP:, :], bank[2][CAP:, :], sil[CAP:, :], ALU.mult).then_inc(drained[2], 1)
                        for n in range(1, PASSES):
                            with dve.If(count > CAP * n):
                                b0 = dve.snap(steps_done)
                                dve.wait_ge(baton, b0)
                                for tt in range(TT):
                                    at_n = place[:, tt, bass.ds(it * 2 + (n * (E + 2) + j), 1)]
                                    v.tensor_scalar(m_selg[n][:, tt, :], iota2, at_n, gates[:, tt, bass.ds(it * 2 + j, 1)], ALU.is_equal, ALU.mult)
                                    ins = v.tensor_scalar(m_sel[:, tt, :], iota, at_n, None, ALU.is_equal)
                                ins.then_inc(baton, 1)
                                dve.wait_ge(baton, b0 + 2)
                                v.tensor_tensor(m_x, bank[4][:, :].rearrange("p (k c) -> p k c", k=KC), columns(g_col, CAP), ALU.mult).then_inc(baton, 1)
                                dve.wait_ge(baton, b0 + 3)
                                v.tensor_tensor(m_x, m_x, columns(b_col, CAP), ALU.add).then_inc(baton, 1)
                                dve.wait_ge(baton, b0 + 6)
                                v.tensor_tensor(m_h[n][CAP:, :], bank[5][CAP:, :], m_sil[CAP:, :], ALU.mult).then_inc(baton, 1)
                                dve.reg_add(steps_done, steps_done, H_STEPS)
                        if j:
                            for g in range(2):
                                dve.wait_ge(filled[g], it + (first[g] + 1))
                                pair_x(g)
                            for g in range(2):
                                dve.wait_ge(x_scaled, it * 2 + ((E + 2) * i + g + 3))
                                pair_x_shift(g)
                        for n in range(1, PASSES):
                            with dve.If(count > CAP * n):
                                b0 = dve.snap(steps_done)
                                dve.wait_ge(baton, b0 + 5)
                                for b in range(4, 8):
                                    dve.wait_ge(drained[b], it + first[b])
                                    ins = v.tensor_tensor(part(b), bank[b][:, :], part(b), ALU.add)
                                ins.then_inc(baton, 1)
                                dve.reg_add(steps_done, steps_done, Y_STEPS)
                    steps = dve.snap(steps_done)
                    dve.wait_ge(baton, steps)
                    for b in range(4, 8):
                        dve.wait_ge(drained[b], it + first[b])
                        dve.wait_ge(filled[b], it + (first[b] + 1))
                        v.tensor_tensor(part(b), bank[b][:, :], part(b), ALU.add).then_inc(drained[b], 1)
                for b in range(4, 8):
                    dve.wait_ge(drained[b], first[b] + E // 2)
                    block_stats(H, (b - 4) // 2, (b - 4) % 2)

            steps_done = dve.alloc_register("steps_done_dve")
            dve.reg_mov(steps_done, 1)
            v.memset(place[:, :, :], -1.0).then_inc(baton, 1)
            dve.wait_ge(baton, 1)
            ht_chunks(0)
            dve.wait_ge(params_in, N_PARAMS)
            ps = wait_data(dve, "cols")
            v.tensor_copy(lncols[:, :], ps[:, 0:P])
            v.tensor_copy(convcols[:, 0, :], ps[:, P:P + 96])
            v.tensor_copy(convcols[:, 1, :], ps[:, 256:352])
            emptied(v.tensor_copy(bscol[:, :], ps[:, 384:392]), "cols")
            wait_copy(dve, "cols")
            nn = 0
            nres = 1
            for i, kind in enumerate(kinds):
                j = kinds[:i].count(kind)
                if kind == 0:
                    delta(i, j)
                    X2 = view(8192, HEADS, P)
                    heads_norm(nn, lambda tt: O[:, :, tt * P:(tt + 1) * P],
                               lambda tt: gate[:, tt, :].rearrange("p (h d) -> p h d", h=HEADS), 1.0)
                    heads_out_T(i, nn, OT)
                    nn += 1
                elif kind == 1:
                    lam_init = 0.8 - 0.6 * math.exp(-0.3 * i)
                    attention(i, j, lam_init)
                    X2 = view(11264, HEADS, P)
                    heads_norm(nn, lambda tt: bO[:, :, tt * P:(tt + 1) * P],
                               lambda tt: bngb[:, :].unsqueeze(1).to_broadcast([P, HEADS, P]), 1.0 - lam_init)
                    heads_out_T(i, nn, bOT)
                    nn += 1
                else:
                    gmlp(i, j)
                dve.wait_ge(h_ready, 2 * nres)
                add_mixed(i)
                layer_norm(2 * i + 1)
                if 2 * i + 1 != last_phase:
                    ht_chunks(2 * i + 1)
                nres += 1
                if with_moe:
                    experts(i, nres)
                    layer_norm(2 * i + 2)
                    nres += 1
                if i < n_layers - 1:
                    ht_chunks(2 * i + 2)

        @block.tensor
        def _(pe):
            mm, tr = nc.tensor.matmul, nc.tensor.transpose
            unit_n = 0

            def fill(*key):
                b, n = at[key]
                if n:
                    pe.wait_ge(drained[b], n)
                return bank[b]

            def done(ins, *key):
                ins.then_inc(filled[at[key][0]], 1)

            def next_unit():
                nonlocal unit_n
                s = unit_n % SLOTS
                pe.wait_ge(slot_in[s], 16 * (unit_n // SLOTS + 1))
                unit_n += 1
                return ring[s]

            def ht_chunks(phase):
                src = XH if phase % 2 else H
                for k in range(KC):
                    ps = fill("ht", phase, k)
                    for tt in range(TT):
                        ins = tr(ps[:, tt * P:(tt + 1) * P], src[:, tt, k * P:(k + 1) * P], ident)
                    done(ins, "ht", phase, k)
                if phase % 2 == 0:
                    for k in range(KC):
                        wait_copy(pe, "ht", phase, k)

            def rows(dst, wt, n):
                for k in range(KC):
                    ins = mm(dst[:, 0:SEQ], wt[:, k, n * P:(n + 1) * P], HT[:, k, :], start=k == 0, stop=k == KC - 1)
                return ins

            def toks(dst, wt, tt):
                for k in range(KC):
                    ins = mm(dst[:, :], HT[:, k, tt * P:(tt + 1) * P], wt[:, k, :], start=k == 0, stop=k == KC - 1)
                return ins

            def heads_out(i, nn, X, XT):
                pss = [fill("oT", i, g) for g in range(4)]
                for tt in range(TT):
                    pe.wait_ge(o_ready, 2 * nn + tt + 1)
                    for g in range(4):
                        for h in (2 * g, 2 * g + 1):
                            c = (h % 2) * SEQ + tt * P
                            ins = tr(pss[g][:, c:c + P], X[:, h, tt * P:(tt + 1) * P], ident)
                        if tt == TT - 1:
                            done(ins, "oT", i, g)
                for g in range(4):
                    wait_copy(pe, "oT", i, g)
                for nh in range(2):
                    wt = next_unit()
                    for tt in range(TT):
                        ps = fill("y", i, tt, nh)
                        for h in range(HEADS):
                            ins = mm(ps[:, :], XT[:, h, tt * P:(tt + 1) * P], wt[:, h, :], start=h == 0, stop=h == HEADS - 1)
                        done(ins, "y", i, tt, nh)

            def delta(i, j):
                ps = fill("ab", i)
                for tt in range(TT):
                    for k in range(KC):
                        ins = mm(ps[:, tt * 16:(tt + 1) * 16], HT[:, k, tt * P:(tt + 1) * P], wab[:, j, k, :], start=k == 0, stop=k == KC - 1)
                done(ins, "ab", i)
                for u in range(6):
                    wt = next_unit()
                    for c in range(4 * u, 4 * u + 4):
                        done(rows(fill("conv", i, c), wt, c % 4), "conv", i, c)
                        if c >= 16:
                            n = c - 16
                            ps = fill("ss", i, n)
                            pe.wait_ge(squares, 8 * j + n + 1)
                            done(mm(ps[:, :], ones[:, :], sq[n % 2], start=True, stop=True), "ss", i, n)
                ps = fill("G", i)
                pe.wait_ge(ab_mid, 2 * j + 2)
                ins = mm(ps[:, 0:16], cum, abr[:, 7, :, :], start=True, stop=True)
                ins = mm(ps[:, 16:32], blk, abr[:, 7, :, :], start=True, stop=True)
                done(ins, "G", i)
                for nh in range(2):
                    wt = next_unit()
                    for tt in range(TT):
                        done(toks(fill("gate", i, tt, nh), wt, tt), "gate", i, tt, nh)
                pe.wait_ge(qk_normed, 8 * j + 8)
                for tt in range(TT):
                    ts = slice(tt * P, (tt + 1) * P)
                    for hg in range(2):
                        ps = fill("GB", i, tt, hg)
                        for h in range(4 * hg, 4 * hg + 4):
                            ins = mm(ps[:, (h % 4) * P:(h % 4 + 1) * P], abr[:, 7, tt, h:h + 1].to_broadcast([P, P]), cum, start=True, stop=True)
                        done(ins, "GB", i, tt, hg)
                    for hg in range(2):
                        for key, right in (("kk", kT), ("qk", qT)):
                            ps = fill(key, i, tt, hg)
                            for h in range(4 * hg, 4 * hg + 4):
                                ins = mm(ps[:, (h % 4) * P:(h % 4 + 1) * P], kT[:, h, ts], right[:, h, ts], start=True, stop=True)
                            done(ins, key, i, tt, hg)
                    pe.wait_ge(silu_qkv, 18 * j + 18)
                    for hg in range(2):
                        for key, src in (("Ktok", kT), ("Vtok", vT)):
                            ps = fill(key, i, tt, hg)
                            for h in range(4 * hg, 4 * hg + 4):
                                ins = tr(ps[:, (h % 4) * P:(h % 4 + 1) * P], src[:, h, ts], ident)
                            done(ins, key, i, tt, hg)
                    for hg in range(2):
                        ps = fill("T0", i, tt, hg)
                        pe.wait_ge(inv_done, 4 * j + 2 * tt + hg + 1)
                        for h in range(4 * hg, 4 * hg + 4):
                            ins = tr(ps[:, (h % 4) * P:(h % 4 + 1) * P], Ti[:, h, :], ident)
                        done(ins, "T0", i, tt, hg)
                    for lv in range(1, LEVELS):
                        for hg in range(2):
                            ps = fill("Y", i, tt, lv, hg)
                            pe.wait_ge(masked, 20 * j + 10 * tt + 2 * (lv - 1) + hg + 1)
                            wait_copy(pe, "T0", i, tt, hg) if lv == 1 else wait_copy(pe, "T", i, tt, lv - 1, hg)
                            for h in range(4 * hg, 4 * hg + 4):
                                ins = mm(ps[:, (h % 4) * P:(h % 4 + 1) * P], AM[:, h, :], T[:, h, :], start=True, stop=True)
                            done(ins, "Y", i, tt, lv, hg)
                        for hg in range(2):
                            wait_copy(pe, "Y", i, tt, lv, hg)
                            if lv > 1:
                                wait_copy(pe, "TT", i, tt, lv - 1, hg)
                            ps = fill("TT", i, tt, lv, hg)
                            for h in range(4 * hg, 4 * hg + 4):
                                ins = mm(ps[:, (h % 4) * P:(h % 4 + 1) * P], Y[:, h, :], Ti[:, h, :], start=True, stop=True)
                            done(ins, "TT", i, tt, lv, hg)
                            if lv < LEVELS - 1:
                                ps = fill("T", i, tt, lv, hg)
                                for h in range(4 * hg, 4 * hg + 4):
                                    ins = mm(ps[:, (h % 4) * P:(h % 4 + 1) * P], Ti[:, h, :], Y[:, h, :], start=True, stop=True)
                                done(ins, "T", i, tt, lv, hg)
                    for hg in range(2):
                        ps = fill("W", i, tt, hg)
                        pe.wait_ge(kscaled, 4 * j + 2 * tt + hg + 1)
                        wait_copy(pe, "TT", i, tt, LEVELS - 1, hg)
                        for h in range(4 * hg, 4 * hg + 4):
                            ins = mm(ps[:, (h % 4) * P:(h % 4 + 1) * P], kG[:, h, :], Ti[:, h, :], start=True, stop=True)
                        done(ins, "W", i, tt, hg)
                    wait_copy(pe, "Vtok", i, tt, 0)
                    wait_copy(pe, "Vtok", i, tt, 1)
                    for hg in range(2):
                        fill("o", i, tt, hg)
                    pe.wait_ge(qdec, 4 * j + 2 * tt + 2)
                    for c in range(2):
                        rr = slice(64 * c, 64 * c + 64)
                        last = (tt, c) == (TT - 1, 1)
                        for hg in range(2):
                            ps = fill("vn", i, tt, c, hg)
                            po = bank[at[("o", i, tt, hg)][0]]
                            if c == 0:
                                for h in range(4 * hg, 4 * hg + 4):
                                    ins = mm(ps[:, (h % 4) * P:(h % 4 + 1) * P], Ti[:, h, :], Vtok[:, h, :], start=h % 4 == 0, stop=False, skip_group_check=True)
                                wait_copy(pe, "W", i, tt, hg)
                            if (tt, c) != (0, 0):
                                wait_copy(pe, "su", i, *((tt, 0) if c else (tt - 1, 1)), hg)
                            for h in range(4 * hg, 4 * hg + 4):
                                mm(po[rr, (h % 4) * P:(h % 4 + 1) * P], qT[:, h, tt * P + 64 * c:tt * P + 64 * c + 64], S[:, h, :],
                                   start=h % 4 == 0, stop=False, skip_group_check=True)
                            for h in range(4 * hg, 4 * hg + 4):
                                ins = mm(ps[rr, (h % 4) * P:(h % 4 + 1) * P], NWT[:, h, rr], S[:, h, :], start=False, stop=True, skip_group_check=True)
                            done(ins, "vn", i, tt, c, hg)
                        for hg in range(2):
                            wait_copy(pe, "vn", i, tt, c, hg)
                            if last:
                                continue
                            ps = fill("su", i, tt, c, hg)
                            pe.wait_ge(kd_ready, 4 * j + 2 * tt + hg + 1)
                            for h in range(4 * hg, 4 * hg + 4):
                                ins = mm(ps[:, (h % 4) * P:(h % 4 + 1) * P], kd[rr, h, :], vnew[rr, h, :], start=True, stop=True)
                            done(ins, "su", i, tt, c, hg)
                    for hg in range(2):
                        po = bank[at[("o", i, tt, hg)][0]]
                        wait_copy(pe, "qk", i, tt, hg)
                        for h in range(4 * hg, 4 * hg + 4):
                            ins = mm(po[:, (h % 4) * P:(h % 4 + 1) * P], attnT[:, h, :], vnew[:, h, :], start=False, stop=True, skip_group_check=True)
                        done(ins, "o", i, tt, hg)

            def attention(i, j):
                for u in range(4):
                    wt = next_unit()
                    for c in range(4 * u, 4 * u + 4):
                        done(rows(fill("qkT", i, c), wt, c % 4), "qkT", i, c)
                        if 4 <= c < 10:
                            n = c - 4
                            if n == 0:
                                pe.wait_ge(toep_in, 48)
                            done(mm(fill("flip", i, n)[:, :], flip, TBr[:, n * 512:(n + 1) * 512], start=True, stop=True), "flip", i, n)
                for nh in range(2):
                    wt = next_unit()
                    for tt in range(TT):
                        done(toks(fill("v", i, tt, nh), wt, tt), "v", i, tt, nh)
                for c in range(16):
                    wait_copy(pe, "qkT", i, c)
                for nh in range(2):
                    for tt in range(TT):
                        wait_copy(pe, "v", i, tt, nh)
                for h in range(-2, HEADS + 1):
                    if 0 <= h < HEADS:
                        ps = fill("pT", i, h)
                        pe.wait_ge(pa_ready, HEADS * j + h + 1)
                        for b in range(3):
                            ins = tr(ps[:, b * P:(b + 1) * P], PA[h % 2][:, b * P:(b + 1) * P], ident)
                        done(ins, "pT", i, h)
                    if h + 2 < HEADS:
                        g = h + 2
                        for m in range(2):
                            ps = fill("lg", i, g, m)
                            ms = slice(64 * m, 64 * m + 64)
                            mm(ps[:, 0:P], qT[ms, g, 0:P], kT[ms, g, 0:P], start=True, stop=True)
                            done(mm(ps[:, P:TOEP], qT[ms, g, P:SEQ], kT[ms, g, :], start=True, stop=True), "lg", i, g, m)
                    if h >= 1:
                        g = h - 1
                        ps = fill("ob", i, g)
                        wait_copy(pe, "pT", i, g)
                        gs = slice(g * P, (g + 1) * P)
                        mm(ps[:, 0:P], PT[g % 2][:, 0:P], Vb[:, 0, gs], start=True, stop=True)
                        mm(ps[:, P:SEQ], PT[g % 2][:, P:2 * P], Vb[:, 0, gs], start=True, stop=False)
                        done(mm(ps[:, P:SEQ], PT[g % 2][:, 2 * P:TOEP], Vb[:, 1, gs], start=False, stop=True), "ob", i, g)

            def gmlp(i, j):
                for u in (4, 5, 6, 7, 0, 1, 2, 3):
                    wt = next_unit()
                    for tt in range(TT):
                        done(toks(fill("z", i, u, tt), wt, tt), "z", i, u, tt)
                    if u == 7:
                        pe.wait_ge(cpar_in, 48)
                        for g in range(2):
                            ps = fill("wsT", i, g)
                            for n in range(4):
                                ins = tr(ps[:, n * P:(n + 1) * P], ws[:, 4 * g + n, :], ident)
                            done(ins, "wsT", i, g)
                for g in range(2):
                    wait_copy(pe, "wsT", i, g)
                for tt in range(TT):
                    pe.wait_ge(v_ln, 2 * j + tt + 1)
                    for g2 in range(4):
                        ps = fill("mix", i, tt, g2)
                        for g in (2 * g2, 2 * g2 + 1):
                            ins = mm(ps[:, (g % 2) * 256:(g % 2 + 1) * 256], wsT[:, g, :], v_[:, tt, g * 256:(g + 1) * 256], start=True, stop=True)
                        done(ins, "mix", i, tt, g2)
                for tt in range(TT):
                    for g2 in range(4):
                        wait_copy(pe, "mix", i, tt, g2)
                for g in range(8):
                    ps = fill("uT", i, g)
                    for n in range(2):
                        for tt in range(TT):
                            c = n * SEQ + tt * P
                            ins = tr(ps[:, c:c + P], u_[:, tt, (2 * g + n) * P:(2 * g + n + 1) * P], ident)
                    done(ins, "uT", i, g)
                for g in range(8):
                    wait_copy(pe, "uT", i, g)
                for nh in range(2):
                    pss = [fill("y", i, tt, nh) for tt in range(TT)]
                    wts = [next_unit(), next_unit()]
                    for tt in range(TT):
                        for k in range(16):
                            ins = mm(pss[tt][:, :], uT[:, k, tt * P:(tt + 1) * P], wts[k // 8][:, k % 8, :], start=k == 0, stop=k == 15)
                        done(ins, "y", i, tt, nh)

            def experts(i):
                nonlocal unit_n
                ps = fill("rt", i)
                for k in range(KC):
                    wait_copy(pe, "ht", 2 * i + 1, k)
                    for tt in range(TT):
                        ins = mm(ps[:, tt * E:(tt + 1) * E], HT[:, k, tt * P:(tt + 1) * P], wr[:, k, :],
                                 start=k == 0 and tt == 0, stop=k == KC - 1, skip_group_check=True)
                done(ins, "rt", i)
                ps = fill("rank", i)
                pe.wait_ge(mask_ready, i + 1)
                mask = [rt[:, 7, tt * E:(tt + 1) * E] for tt in range(TT)]
                mm(ps[:, 0:E], tri, mask[0], start=True, stop=True)
                for col, last in ((E, tri), (2 * E, ones[:, :])):
                    mm(ps[:, col:col + E], ones[:, :], mask[0], start=True, stop=False)
                    ins = mm(ps[:, col:col + E], last, mask[1], start=False, stop=True)
                done(ins, "rank", i)

                def gather(g):
                    for k in range(4):
                        for tt in range(TT):
                            ins = mm(bank[g][:, k * 2 * CAP:(k + 1) * 2 * CAP], XH[:, tt, (4 * g + k) * P:(4 * g + k + 1) * P], sel[:, tt, :],
                                     start=tt == 0, stop=tt == TT - 1)
                    return ins

                def up(b, x, w1, w3):
                    for k in range(KC):
                        for lo, wt in ((0, w1), (CAP, w3)):
                            ins = mm(bank[b][lo:lo + CAP, :], x[:, k, :], wt[:, k, :], start=k == 0, stop=k == KC - 1, skip_group_check=True)
                    return ins

                def turn(b, columns, h):
                    for n, tile in enumerate(columns):
                        tr(bank[b][:, n * P:(n + 1) * P], tile, ident)
                    for m in range(4):
                        c = SEQ + m * CAP
                        ins = tr(bank[b][:, c:c + CAP], h[CAP:, m * P:(m + 1) * P], ident[CAP:, CAP:])
                    return ins

                def down(b, h, w2):
                    for m in range(4):
                        for nh in range(2):
                            ins = mm(bank[b][nh * CAP:(nh + 1) * CAP, :], h[:, m, :], w2[:, m, nh * 512:(nh + 1) * 512],
                                     start=m == 0, stop=m == 3, skip_group_check=True)
                    return ins

                first = at[("moe", i)]
                pe.wait_ge(sel_ready, (E // 2 + 1) * i + 1)
                for g in range(2):
                    fill("first", i, g)
                    done(gather(g), "first", i, g)
                wait_copy(pe, "rank", i)
                with pe.Fori(0, E // 2) as it:
                    for j in range(2):
                        s1, s3, s2 = [(unit_n + 3 * j + n) % SLOTS for n in range(3)]
                        c1, c3, c2 = [(unit_n + 3 * j + n) // SLOTS for n in range(3)]
                        w2 = ring[s2][:, :, :].rearrange("p a b -> p (a b)").rearrange("p (m n) -> p m n", m=4)
                        count = pe.value_load(counts[0:1, bass.ds(it * 2 + j, 1)], min_val=0, max_val=SEQ)

                        def free(b, n):
                            pe.wait_ge(drained[b], it * PAIR_TURNS[b] + (first[b] + n))

                        if not j:
                            free(0, 0)
                            free(1, 0)
                        pe.wait_ge(slot_in[s1], it * 16 + 16 * (c1 + 1))
                        pe.wait_ge(slot_in[s3], it * 16 + 16 * (c3 + 1))
                        free(2, 2 * j)
                        up(2, x_[:, :, CAP * j:CAP * (j + 1)], ring[s1], ring[s3]).then_inc(filled[2], 1)
                        if not j:
                            pe.wait_ge(sel_ready, it + ((E // 2 + 1) * i + 2))
                        gather(j).then_inc(filled[j], 1)
                        for n in range(1, PASSES):
                            with pe.If(count > CAP * n):
                                b0 = pe.snap(steps_done)
                                free(4, 0)
                                free(5, 0)
                                pe.wait_ge(baton, b0 + 1)
                                for k in range(KC):
                                    for tt in range(TT):
                                        ins = mm(bank[4][:, k * CAP:(k + 1) * CAP], XH[:, tt, k * P:(k + 1) * P], m_sel[:, tt, :], start=tt == 0, stop=tt == TT - 1)
                                ins.then_inc(baton, 1)
                                pe.wait_ge(baton, b0 + 4)
                                up(5, m_x, ring[s1], ring[s3]).then_inc(baton, 1)
                                pe.reg_add(steps_done, steps_done, H_STEPS)
                        free(2, 2 * j + 1)
                        turn(2, [selg[:, j, :]], h_).then_inc(filled[2], 1)
                        pe.wait_ge(slot_in[s2], it * 16 + 16 * (c2 + 1))
                        free(2, 2 * j + 2)
                        free(3, j)
                        for n in range(1, PASSES):
                            with pe.If(count > CAP * n):
                                b0 = pe.snap(steps_done)
                                for b in range(4, 8):
                                    free(b, 0)
                                pe.wait_ge(baton, b0)
                                turn(6, [m_selg[n][:, tt, :] for tt in range(TT)], m_h[n]).then_inc(baton, 1)
                                pe.wait_ge(baton, b0 + 2)
                                down(7, m_turned[:, SEQ:].rearrange("p (m c) -> p m c", m=4), w2).then_inc(baton, 1)
                                pe.wait_ge(baton, b0 + 4)
                                for tt in range(TT):
                                    for nh in range(2):
                                        rr = slice(nh * CAP, (nh + 1) * CAP)
                                        ins = mm(bank[4 + 2 * tt + nh][:, :], m_turned[rr, tt * P:(tt + 1) * P], m_y[rr, :], start=True, stop=True)
                                ins.then_inc(baton, 1)
                                pe.reg_add(steps_done, steps_done, Y_STEPS)
                        down(3, hT, w2).then_inc(filled[3], 1)
                    steps = pe.snap(steps_done)
                    pe.wait_ge(baton, steps)
                    free(3, 2)
                    for tt in range(TT):
                        for nh in range(2):
                            b = 4 + 2 * tt + nh
                            free(b, 0)
                            mm(bank[b][:, :], selgT[:, tt * P:(tt + 1) * P], y_[:, nh * 512:(nh + 1) * 512], start=True, stop=True).then_inc(filled[b], 1)
                unit_n += 3 * E

            steps_done = pe.alloc_register("steps_done_pe")
            pe.reg_mov(steps_done, 1)
            pe.wait_ge(masks_in, 16)
            pe.wait_ge(x_ready, 16)
            ht_chunks(0)
            pe.wait_ge(params_in, N_PARAMS)
            pe.wait_ge(consts_set, 4)
            ps = fill("cols")
            tr(ps[:, 0:P], lnrows[:, :], ident)
            for j in range(2):
                tr(ps[:, P * (j + 1):P * (j + 1) + 96], convrows[:, j, :], ident[0:96, 0:96])
            done(tr(ps[:, 384:392], bsrow[:, :], ident[0:HEADS, 0:HEADS]), "cols")
            done(mm(fill("relrow")[0:HEADS, 0:TOEP], rel33[:, :], onehot, start=True, stop=True), "relrow")
            nn = 0
            lnn = 0
            for i, kind in enumerate(kinds):
                j = kinds[:i].count(kind)
                if kind == 0:
                    delta(i, j)
                    heads_out(i, nn, O, OT)
                    nn += 1
                elif kind == 1:
                    attention(i, j)
                    heads_out(i, nn, bO, bOT)
                    nn += 1
                else:
                    gmlp(i, j)
                lnn += 1
                if 2 * i + 1 != last_phase:
                    pe.wait_ge(xhat_ready, 2 * lnn)
                    ht_chunks(2 * i + 1)
                if with_moe:
                    experts(i)
                    lnn += 1
                if i < n_layers - 1:
                    if with_moe:
                        pe.wait_ge(xhat_ready, 2 * lnn)
                    ht_chunks(2 * i + 2)


N_PARAMS = 16 * 21


def constants():
    import numpy as np

    c = np.zeros((P, C_ALL), np.float32)
    m, t = np.arange(P)[:, None], np.arange(P)[None, :]
    same = m // CHUNK == t // CHUNK
    c[:, C_ID:C_ID + P] = m == t
    c[:, C_NEG:C_NEG + P] = np.where(same & (t >= m), 0.0, -BIG)
    for lv in range(LEVELS):
        b = 1 << lv
        c[:, C_LV + lv * P:C_LV + (lv + 1) * P] = (m // (2 * b) == t // (2 * b)) & (m // b % 2 == 0) & (t // b % 2 == 1)
    c[:, C_CUM:C_CUM + P] = same & (m <= t)
    c[:, C_BLK:C_BLK + P] = same
    c[:, C_TRI:C_TRI + P] = m <= t
    exact = REL_BUCKETS // 2
    n = 255 - np.arange(TOEP)
    large = exact + (np.log(np.maximum(n, 1).astype(np.float32) / np.float32(exact)) / np.float32(math.log(128 / exact))
                     * np.float32(REL_BUCKETS - exact)).astype(np.int32)
    bucket = np.where(n < 0, REL_BUCKETS, np.where(n < exact, np.maximum(n, 0), np.minimum(large, REL_BUCKETS - 1)))
    c[bucket, C_OH + np.arange(TOEP)] = 1.0
    c[:, C_FLIP:C_FLIP + P] = m + t == P - 1
    c[:, C_CD:C_CD + E] = E - np.arange(E)
    c[:, C_IOTA:C_IOTA + 2 * CAP] = np.arange(2 * CAP) % CAP
    return c


_INS = ["x", "ln_mix_g", "ln_mix_b", "ln_ffn_g", "ln_ffn_b", "a_w_in", "a_conv", "a_a_log", "a_dt_bias", "a_norm_g",
        "a_w_out", "b_w_in", "b_lambda", "b_norm_g", "b_w_out", "rel_bias", "c_w_in", "c_ln_g", "c_ln_b", "c_w_s",
        "c_b_s", "c_w_out", "w_router", "router_bias", "e_w1", "e_w3", "e_w2"]


def kernel(**inputs):
    import numpy as np
    import concourse.bacc as bacc
    from concourse.bass_utils import run_bass_kernel_spmd

    nc = bacc.Bacc("TRN2", target_bir_lowering=False, num_devices=1)
    arrays = {f"in_{name}": np.ascontiguousarray(inputs[name]) for name in _INS}
    arrays["in_consts"] = constants()
    w = {name[3:]: nc.dram_tensor(name, a.shape, mybir.dt.from_np(a.dtype), kind="ExternalInput").ap()
         for name, a in arrays.items()}
    out = nc.dram_tensor("out", [1, SEQ, D], F32, kind="ExternalOutput").ap()
    trunk(nc, w, out)
    r = run_bass_kernel_spmd(nc, [arrays], core_ids=[0])
    return r.results[0]["out"]
```
